# Optimizing a Trainium2 kernel written in Bass

```python
import jax, jax.numpy as jnp
from jax import lax
import numpy as np

D_MODEL = 1024
BATCH = 1
SEQ = 128
DEPTH = 1
DEC_BATCH = 1
DEC_SEQ = 512
PAST_LEN = 128

GRID_W = 64
HEAD_DIM = 64
N_Q_HEADS = 8
N_KV_HEADS = 2
GQA_GROUP = N_Q_HEADS // N_KV_HEADS
D_ATTN = N_Q_HEADS * HEAD_DIM
D_KV = N_KV_HEADS * HEAD_DIM
RWKV_HEAD = 64
N_RWKV_HEADS = 8
D_RWKV = N_RWKV_HEADS * RWKV_HEAD
DECAY_LORA = 32
AAA_LORA = 32
GATE_LORA = 96
D_RWKV_IN = 3 * D_RWKV + 2 * DECAY_LORA + 2 * AAA_LORA + GATE_LORA
D_IN = D_ATTN + 2 * D_KV + D_RWKV_IN
D_MIX = D_ATTN + D_RWKV
RWKV_SPLITS = [D_RWKV, 2 * D_RWKV, 3 * D_RWKV, 3 * D_RWKV + 2 * DECAY_LORA, 3 * D_RWKV + 2 * DECAY_LORA + 2 * AAA_LORA]
N_GROUPS = 4
EXPERTS_PER_GROUP = 4
N_EXPERTS = N_GROUPS * EXPERTS_PER_GROUP
TOP_K_FINE = 2
D_EXPERT = 512
Q_BLOCK = 128
ROPE_THETA = 10000.0
NORM_EPS = 1e-6
GN_EPS = 64e-5
DECAY_SCALE = 0.6065306597

kernel_name = 'hymba_gqa_rwkv7_hmoe_diffusion_step'

def rms_norm(x, g):
    xf = x.astype(jnp.float32)
    y = xf * lax.rsqrt(jnp.mean(xf * xf, axis=-1, keepdims=True) + NORM_EPS)
    return (y * g.astype(jnp.float32)).astype(x.dtype)

def modulate(x, g, shift, scale):
    return rms_norm(x, g) * (1 + scale[:, None, :]) + shift[:, None, :]

def rope_2d(x, row, col):
    half = HEAD_DIM // 2
    inv = ROPE_THETA ** (-jnp.arange(0, half, 2, dtype=jnp.float32) / half)

    def rot(xa, pos):
        ang = pos.astype(jnp.float32)[:, None] * inv[None, :]
        cos, sin = jnp.cos(ang), jnp.sin(ang)
        x1, x2 = jnp.split(xa.astype(jnp.float32), 2, axis=-1)
        return jnp.concatenate([x1 * cos - x2 * sin, x1 * sin + x2 * cos], axis=-1)

    return jnp.concatenate([rot(x[..., :half], row), rot(x[..., half:], col)], axis=-1).astype(x.dtype)

def block_attention(q, k, v):
    B, Hk, G, Tq, hd = q.shape
    nb = Tq // Q_BLOCK
    qb = jnp.moveaxis(q.reshape(B, Hk, G, nb, Q_BLOCK, hd), 3, 0)
    scale = HEAD_DIM ** -0.5

    def one(qblk):
        s = jnp.einsum('bkgqd,bksd->bkgqs', qblk, k).astype(jnp.float32) * scale
        p = jax.nn.softmax(s, axis=-1).astype(v.dtype)
        return jnp.einsum('bkgqs,bksd->bkgqd', p, v)

    ob = lax.map(one, qb)
    return jnp.moveaxis(ob, 0, 3).reshape(B, Hk, G, Tq, hd)

def centred_shift(p, mu):
    zero = jnp.zeros_like(p[:, :1])
    prev = jnp.concatenate([zero, p[:, :-1]], axis=1)
    nxt = jnp.concatenate([p[:, 1:], zero], axis=1)
    return p + mu[0] * (prev - p) + mu[1] * (nxt - p)

def rwkv7_scan(r, w, k, v, kk, b, s0, reverse):
    def step(S, inp):
        r_t, w_t, k_t, v_t, kk_t, b_t = inp
        sa = jnp.einsum('bhvk,bhk->bhv', S, kk_t)
        S = S * w_t[:, :, None, :] - sa[..., None] * b_t[:, :, None, :] + v_t[..., None] * k_t[:, :, None, :]
        return S, jnp.einsum('bhvk,bhk->bhv', S, r_t)

    xs = tuple(jnp.moveaxis(a, 1, 0) for a in (r, w, k, v, kk, b))
    S, y = lax.scan(step, s0, xs, reverse=reverse)
    return jnp.moveaxis(y, 0, 1), S

def rwkv7_group(rw, lp, ctx_state):
    B, T, _ = rw.shape
    f32 = jnp.float32
    hd = lambda t: t.reshape(B, T, N_RWKV_HEADS, RWKV_HEAD)
    rw = centred_shift(rw, lp['mu_shift'])
    r, k, v, wd, ad, gd = jnp.split(rw, RWKV_SPLITS, axis=-1)
    decay_logit = lp['w0'] + jnp.einsum('btzl,zlc->btzc', jnp.tanh(wd.reshape(B, T, 2, DECAY_LORA)), lp['w_lora_up'])
    decay = jnp.exp(-DECAY_SCALE * jax.nn.sigmoid(decay_logit.astype(f32)))
    a = jax.nn.sigmoid((lp['a0'] + jnp.einsum('btzl,zlc->btzc', ad.reshape(B, T, 2, AAA_LORA), lp['a_lora_up'])).astype(f32))
    g = jnp.einsum('btl,lc->btc', jax.nn.sigmoid(gd), lp['g_lora_up']).astype(f32)
    r, k, v = r.astype(f32), k.astype(f32), v.astype(f32)
    kk = hd(k * lp['k_k'].astype(f32))
    kk = (kk * lax.rsqrt(jnp.sum(kk * kk, axis=-1, keepdims=True) + 1e-12)).reshape(B, T, D_RWKV)
    k_dir = k[:, :, None, :] * (1.0 + (a - 1.0) * lp['k_a'].astype(f32))
    b_dir = kk[:, :, None, :] * a
    if ctx_state is None:
        s0 = jnp.zeros((B, 2, N_RWKV_HEADS, RWKV_HEAD, RWKV_HEAD), f32)
    else:
        s0 = ctx_state.astype(f32)
    y_f, s_f = rwkv7_scan(hd(r), hd(decay[:, :, 0]), hd(k_dir[:, :, 0]), hd(v), hd(kk), hd(b_dir[:, :, 0]), s0[:, 0], False)
    y_b, s_b = rwkv7_scan(hd(r), hd(decay[:, :, 1]), hd(k_dir[:, :, 1]), hd(v), hd(kk), hd(b_dir[:, :, 1]), s0[:, 1], True)
    y = y_f + y_b
    mean = jnp.mean(y, axis=-1, keepdims=True)
    var = jnp.mean(jnp.square(y - mean), axis=-1, keepdims=True)
    y = ((y - mean) * lax.rsqrt(var + GN_EPS)).reshape(B, T, D_RWKV) * lp['ln_x_g'].astype(f32) + lp['ln_x_b'].astype(f32)
    bonus = jnp.sum(hd(r * k) * lp['r_k'].astype(f32), axis=-1, keepdims=True) * hd(v)
    y = (y + bonus.reshape(B, T, D_RWKV)) * g
    return y.astype(rw.dtype), jnp.stack([s_f, s_b], axis=1)

def token_mixer(h, lp, row, col, ctx_k, ctx_v, ctx_state):
    B, T, _ = h.shape
    proj = jnp.einsum('btd,de->bte', h, lp['w_in'])
    q, k, v, rw = jnp.split(proj, [D_ATTN, D_ATTN + D_KV, D_ATTN + 2 * D_KV], axis=-1)
    q = rms_norm(q.reshape(B, T, N_Q_HEADS, HEAD_DIM), lp['q_norm_g']).transpose(0, 2, 1, 3)
    k = rms_norm(k.reshape(B, T, N_KV_HEADS, HEAD_DIM), lp['k_norm_g'])
    v = v.reshape(B, T, N_KV_HEADS, HEAD_DIM)
    if ctx_k is None:
        keys, vals = k.transpose(0, 2, 1, 3), v.transpose(0, 2, 1, 3)
    else:
        q = rope_2d(q, row, col)
        keys = jnp.concatenate([rope_2d(k.transpose(0, 2, 1, 3), row, col), ctx_k.astype(k.dtype).transpose(0, 2, 1, 3)], axis=2)
        vals = jnp.concatenate([v.transpose(0, 2, 1, 3), ctx_v.astype(v.dtype).transpose(0, 2, 1, 3)], axis=2)
    o = block_attention(q.reshape(B, N_KV_HEADS, GQA_GROUP, T, HEAD_DIM), keys, vals)
    attn_out = o.reshape(B, N_Q_HEADS, T, HEAD_DIM).transpose(0, 2, 1, 3).reshape(B, T, D_ATTN)
    rwkv_out, state = rwkv7_group(rw, lp, ctx_state)
    out = jnp.einsum('btc,cd->btd', jnp.concatenate([attn_out, rwkv_out], axis=-1), lp['w_out'])
    return out, (k, v, state)

def hier_moe(h, lp):
    B, T, D = h.shape
    f32 = jnp.float32
    x = h.reshape(B * T, D)
    lc = jnp.einsum('nd,dg->ng', x, lp['router_c']).astype(f32) + lp['router_c_b'].astype(f32)
    pc = jax.nn.softmax(lc, axis=-1)
    g_idx = jnp.argmax(lc, axis=-1)
    g_hot = jax.nn.one_hot(g_idx, N_GROUPS, dtype=f32)
    g_w = jnp.sum(pc * g_hot, axis=-1, keepdims=True)
    lf = (jnp.einsum('nd,de->ne', x, lp['router_f']).astype(f32) + lp['router_f_b'].astype(f32)).reshape(-1, N_GROUPS, EXPERTS_PER_GROUP)
    lf_sel = jnp.einsum('nge,ng->ne', lf, g_hot)
    top_w, top_i = lax.top_k(jax.nn.softmax(lf_sel, axis=-1), TOP_K_FINE)
    top_w = top_w / jnp.sum(top_w, axis=-1, keepdims=True)
    expert_id = g_idx[:, None] * EXPERTS_PER_GROUP + top_i
    combine = jnp.sum(jax.nn.one_hot(expert_id, N_EXPERTS, dtype=f32) * (g_w * top_w)[..., None], axis=1)
    out = jnp.zeros_like(x)
    for e in range(N_EXPERTS):
        hid = jax.nn.silu(x @ lp['exp_gate'][e]) * (x @ lp['exp_up'][e])
        out = out + combine[:, e:e + 1].astype(x.dtype) * (hid @ lp['exp_down'][e])
    return out.reshape(B, T, D)

def trunk_layer(x, cond, lp, row, col, ctx_k, ctx_v, ctx_state):
    mod = jnp.einsum('bd,de->be', jax.nn.silu(cond), lp['w_mod']) + lp['b_mod']
    sh1, sc1, g1, sh2, sc2, g2 = jnp.split(mod, 6, axis=-1)
    mix, ctx_out = token_mixer(modulate(x, lp['norm1_g'], sh1, sc1), lp, row, col, ctx_k, ctx_v, ctx_state)
    x = x + g1[:, None, :] * mix
    x = x + g2[:, None, :] * hier_moe(modulate(x, lp['norm2_g'], sh2, sc2), lp)
    return x, ctx_out

def setup_inputs(seed: int = 0) -> dict:
    key = jax.random.key(seed)
    ks = iter(jax.random.split(key, 48))
    f32 = jnp.float32
    nrm = lambda shape, s: jax.random.normal(next(ks), shape, f32) * s
    D, L = D_MODEL, DEPTH
    return {
        'x_prompt': nrm((BATCH, SEQ, D), 1.0),
        'x_sample': nrm((DEC_BATCH, DEC_SEQ, D), 1.0),
        'cache_k': nrm((DEC_BATCH, L, PAST_LEN, N_KV_HEADS, HEAD_DIM), 1.0),
        'cache_v': nrm((DEC_BATCH, L, PAST_LEN, N_KV_HEADS, HEAD_DIM), 1.0),
        'state_rwkv': nrm((DEC_BATCH, L, 2, N_RWKV_HEADS, RWKV_HEAD, RWKV_HEAD), 0.3),
        'c': nrm((DEC_BATCH, D), 1.0),
        'c_ctx': nrm((D,), 1.0),
        'w_mod': nrm((L, D, 6 * D), D ** -0.5),
        'b_mod': nrm((L, 6 * D), 0.02),
        'norm1_g': 1.0 + nrm((L, D), 0.02),
        'norm2_g': 1.0 + nrm((L, D), 0.02),
        'w_in': nrm((L, D, D_IN), D ** -0.5),
        'mu_shift': jax.random.uniform(next(ks), (L, 2, D_RWKV_IN), f32, 0.0, 0.5),
        'q_norm_g': 1.0 + nrm((L, HEAD_DIM), 0.02),
        'k_norm_g': 1.0 + nrm((L, HEAD_DIM), 0.02),
        'w0': nrm((L, 2, D_RWKV), 0.5),
        'w_lora_up': nrm((L, 2, DECAY_LORA, D_RWKV), DECAY_LORA ** -0.5),
        'a0': nrm((L, 2, D_RWKV), 0.5),
        'a_lora_up': nrm((L, 2, AAA_LORA, D_RWKV), AAA_LORA ** -0.5),
        'g_lora_up': nrm((L, GATE_LORA, D_RWKV), GATE_LORA ** -0.5),
        'k_k': 0.85 + nrm((L, D_RWKV), 0.02),
        'k_a': 1.0 + nrm((L, D_RWKV), 0.02),
        'r_k': nrm((L, N_RWKV_HEADS, RWKV_HEAD), 0.1),
        'ln_x_g': 1.0 + nrm((L, D_RWKV), 0.02),
        'ln_x_b': nrm((L, D_RWKV), 0.02),
        'w_out': nrm((L, D_MIX, D), D_MIX ** -0.5),
        'router_c': nrm((L, D, N_GROUPS), D ** -0.5),
        'router_c_b': nrm((L, N_GROUPS), 0.01),
        'router_f': nrm((L, D, N_EXPERTS), D ** -0.5),
        'router_f_b': nrm((L, N_EXPERTS), 0.01),
        'exp_gate': nrm((L, N_EXPERTS, D, D_EXPERT), D ** -0.5),
        'exp_up': nrm((L, N_EXPERTS, D, D_EXPERT), D ** -0.5),
        'exp_down': nrm((L, N_EXPERTS, D_EXPERT, D), D_EXPERT ** -0.5),
    }

def reference(x_prompt, x_sample, cache_k, cache_v, state_rwkv, c, c_ctx, w_mod, b_mod, norm1_g, norm2_g, w_in, mu_shift, q_norm_g, k_norm_g, w0, w_lora_up, a0, a_lora_up, g_lora_up, k_k, k_a, r_k, ln_x_g, ln_x_b, w_out, router_c, router_c_b, router_f, router_f_b, exp_gate, exp_up, exp_down):
    rows = x_sample.shape[1] // GRID_W
    row = jnp.repeat(jnp.arange(rows, dtype=jnp.int32), GRID_W)
    col = jnp.tile(jnp.arange(GRID_W, dtype=jnp.int32), rows)
    cond_ctx = c_ctx[None, :]
    y_prompt, y_sample = x_prompt, x_sample
    ks, vs, ss = [], [], []
    for l in range(DEPTH):
        lp = dict(w_mod=w_mod[l], b_mod=b_mod[l], norm1_g=norm1_g[l], norm2_g=norm2_g[l], w_in=w_in[l],
                  mu_shift=mu_shift[l], q_norm_g=q_norm_g[l], k_norm_g=k_norm_g[l], w0=w0[l], w_lora_up=w_lora_up[l],
                  a0=a0[l], a_lora_up=a_lora_up[l], g_lora_up=g_lora_up[l], k_k=k_k[l], k_a=k_a[l], r_k=r_k[l],
                  ln_x_g=ln_x_g[l], ln_x_b=ln_x_b[l], w_out=w_out[l], router_c=router_c[l], router_c_b=router_c_b[l],
                  router_f=router_f[l], router_f_b=router_f_b[l], exp_gate=exp_gate[l], exp_up=exp_up[l], exp_down=exp_down[l])
        y_prompt, (k_l, v_l, s_l) = trunk_layer(y_prompt, cond_ctx, lp, None, None, None, None, None)
        ks.append(k_l)
        vs.append(v_l)
        ss.append(s_l)
        y_sample, _ = trunk_layer(y_sample, c, lp, row, col, cache_k[:, l], cache_v[:, l], state_rwkv[:, l])
    new_cache_k = jnp.stack(ks, axis=1)
    new_cache_v = jnp.stack(vs, axis=1)
    new_state_rwkv = jnp.stack(ss, axis=1)
    return (y_prompt, y_sample, new_cache_k, new_cache_v, new_state_rwkv)


_drawn_inputs = setup_inputs


def setup_inputs(seed=0):
    import zlib

    import numpy as np

    out = dict(_drawn_inputs(seed))
    spreads = {}
    factors = {'state_rwkv': 4.462,
     'q_norm_g': 8.0,
     'k_norm_g': 8.276,
     'k_k': 3.271,
     'ln_x_g': 34.895,
     'ln_x_b': 37.06,
     'router_c_b': 28.974,
     'router_f_b': 78.778,
     'cache_k': 8.0,
     'cache_v': 8.0,
     'norm2_g': 4.031}
    for name, (base, spread) in spreads.items():
        noise = np.random.default_rng([zlib.crc32(name.encode()), seed]).standard_normal(out[name].shape)
        drawn = base * np.exp(spread * noise) if base else spread * noise
        out[name] = __import__('jax').numpy.asarray(drawn.astype(out[name].dtype))
    for name, factor in factors.items():
        out[name] = (out[name] * factor).astype(out[name].dtype)
    return out
```

```python
from contextlib import ExitStack

import numpy as np
import concourse.bass as bass
from concourse import mybir

F32 = mybir.dt.float32
I32 = mybir.dt.int32
ACT = mybir.ActivationFunctionType
ALU = mybir.AluOpType
AX = mybir.AxisListType

P = 128
D = 1024
KT = D // P
T_CTX, T_LAT = 128, 512
T = T_CTX + T_LAT
NTT = T // P
HD = 64
NQ, NKV = 8, 2
D_ATTN = NQ * HD
D_KV = NKV * HD
D_QKV = D_ATTN + 2 * D_KV
PAST = 128
D_RWKV = 512
NC4 = D_RWKV // P
LORA_IN = 128
GATE_LORA = 96
NET = 14
C = 64
NCH = T // C
DS = 0.6065306597
LEVELS = 6
NG, EPG, NE = 4, 4, 16
FE = 512
NT = 25
EPS = 1e-6
GN_EPS = 64e-5
GRID_W = 64
BIG = 3.0e38

_CONST = {}


def _const_cols():
    at = 0
    for name, n in (("ident", P), ("istack", C), ("ones", P), ("blockones", P), ("stricttri", P),
                    ("levels", 2 * LEVELS * P), ("mstrict", 2 * C), ("mincl", 2 * C), ("mnegincl", 2 * C),
                    ("rope_c", 4 * HD), ("rope_s", 4 * HD), ("scanmask", T), ("sel", 2 * P),
                    ("prio", 4), ("tile_iota", NT)):
        _CONST[name] = (at, n)
        at += n
    return at


NCONST = _const_cols()


def const_table():
    out = np.zeros((P, NCONST), np.float32)

    def put(name, value):
        a, n = _CONST[name]
        out[:, a:a + n] = np.asarray(value, np.float32).reshape(P, n)

    q = np.arange(P)
    half, pos = q // C, q % C
    put("ident", np.eye(P))
    put("istack", pos[:, None] == np.arange(C)[None])
    put("ones", np.ones((P, P)))
    same = half[:, None] == half[None]
    put("blockones", same)
    put("stricttri", q[:, None] < q[None])
    s, t = pos[:, None], pos[None]
    lev = np.zeros((P, 2, LEVELS, P))
    for j in range(LEVELS):
        m = 2 ** j
        near = same & (s // (2 * m) == t // (2 * m)) & (s // m != t // m)
        lev[:, 0, j] = -1.0 * (near & (t > s))
        lev[:, 1, j] = -1.0 * (near & (t < s))
    put("levels", lev)
    tt = np.arange(C)[None]
    put("mstrict", np.stack([tt > s, tt < s], 1))
    put("mincl", np.stack([tt >= s, tt <= s], 1))
    put("mnegincl", -np.stack([tt >= s, tt <= s], 1).astype(np.float32))
    hh = HD // 2
    inv = (10000.0 ** (-np.arange(0, hh, 2, dtype=np.float32) / hh)).astype(np.float32)
    tok = np.arange(T_LAT)
    rc = np.zeros((T_LAT, HD), np.float32)
    rs = np.zeros((T_LAT, HD), np.float32)
    for g, where in enumerate((tok // GRID_W, tok % GRID_W)):
        ang = where.astype(np.float32)[:, None] * inv[None]
        rc[:, g * hh:(g + 1) * hh] = np.concatenate([np.cos(ang), np.cos(ang)], 1)
        rs[:, g * hh:(g + 1) * hh] = np.concatenate([-np.sin(ang), np.sin(ang)], 1)
    put("rope_c", rc.reshape(4, P, HD).transpose(1, 0, 2))
    put("rope_s", rs.reshape(4, P, HD).transpose(1, 0, 2))
    put("scanmask", np.broadcast_to(np.arange(T) % C != 0, (P, T)))
    sel = np.zeros((P, 2, P))
    sel[0, 0] = 1
    sel[1, 1] = 1
    put("sel", sel)
    put("prio", np.broadcast_to(np.array([4, 3, 2, 1]), (P, 4)))
    put("tile_iota", np.broadcast_to(np.arange(NT), (P, NT)))
    return out


class Chain:

    def __init__(self, eng, sem):
        self.eng, self.sem, self.n = eng, sem, 0

    def __call__(self, ins):
        self.n += 1
        ins.then_inc(self.sem, 1)
        self.eng.wait_ge(self.sem, self.n)


def build(nc, x_prompt, x_sample, cache_k, cache_v, state_rwkv, c, c_ctx, w_mod, b_mod, norm1_g, norm2_g, w_in,
          mu_shift, q_norm_g, k_norm_g, w0, w_lora_up, a0, a_lora_up, g_lora_up, k_k, k_a, r_k, ln_x_g, ln_x_b,
          w_out, router_c, router_c_b, router_f, router_f_b, exp_gate, exp_up, exp_down, consts,
          y_prompt, y_sample, new_cache_k, new_cache_v, new_state):
    ctx = ExitStack()
    with ctx:
        phase_sems = []

        def sem(name):
            one = nc.alloc_semaphore(name)
            phase_sems.append(one)
            return one

        top = [0]
        arena = ctx.enter_context(nc.sbuf_tensor("arena", [P, 53000], F32))
        ps = ctx.enter_context(nc.psum_tensor("ps", [P, 8, 512], F32))

        def view(at, *shape):
            n = int(np.prod(shape))
            assert at + n <= 53000, (at, n)
            v = arena[:, at:at + n]
            if len(shape) == 1:
                return v
            names = "abcdef"[:len(shape)]
            return v.rearrange("p (%s) -> p %s" % (" ".join(names), " ".join(names)), **dict(zip(names, shape)))

        def take(*shape):
            v = view(top[0], *shape)
            top[0] += int(np.prod(shape))
            return v

        const = take(NCONST)

        def cst(name, *shape):
            a, n = _CONST[name]
            v = const[:, a:a + n]
            if len(shape) < 2:
                return v
            names = "abcdef"[:len(shape)]
            return v.rearrange("p (%s) -> p %s" % (" ".join(names), " ".join(names)), **dict(zip(names, shape)))

        ident, istack, ones, blockones = cst("ident"), cst("istack"), cst("ones"), cst("blockones")
        stricttri = cst("stricttri")
        levels = cst("levels", 2, LEVELS, P)
        mstrict, mincl, mnegincl = cst("mstrict", 2, C), cst("mincl", 2, C), cst("mnegincl", 2, C)
        rope_c, rope_s = cst("rope_c", 4, HD), cst("rope_s", 4, HD)
        scanmask, sel = cst("scanmask"), cst("sel", 2, P)
        mu = take(2, NET)
        mu_c0 = take(NET)
        w0v, a0v = take(2, NC4), take(2, NC4)
        kkv, kav, ka1v, rkv, lngv, lnbv = (take(NC4) for _ in range(6))
        gq, gk = take(HD), take(HD)
        lorabd = take(4, D_RWKV)
        glora = take(D_RWKV)
        router = take(KT, NG + NE)
        rbias = take(NG + NE)
        ssq, rstd = take(NTT), take(NTT)
        pc_all = take(2, NC4, NCH)
        wsel = take(2, NTT)
        slot_f = take(2, NTT)
        cond2 = take(KT, 2)
        slot_i = ctx.enter_context(nc.sbuf_tensor("slot_i", [P, 2 * NTT], I32))
        eid_i = ctx.enter_context(nc.sbuf_tensor("eid_i", [P, NT], I32))
        CB = top[0]

        rws = view(CB, NET, T)
        qkv = view(CB + NET * T, NTT, D_QKV)
        R = CB + NET * T + NTT * D_QKV

        attn_d = nc.dram_tensor("attn_scratch", (P, NC4 * T), F32, kind="Internal").ap()
        bonus_d = nc.dram_tensor("bonus_scratch", (P, NC4 * T), F32, kind="Internal").ap()
        xg_d = nc.dram_tensor("gathered_tokens", ((NT + 1) * P, D), F32, kind="Internal").ap()
        yg_d = nc.dram_tensor("expert_outputs", (NT * P, D), F32, kind="Internal").ap()

        at = R
        xs = view(at, NTT, D); at += NTT * D
        shift1 = view(at, 2, D); gain1 = view(at + 2 * D, 2, D); at += 4 * D
        ring = view(at, 3, KT, 512); at += 3 * KT * 512
        hT = view(at, KT, T); at += KT * T
        htmp = view(at, 2, D); at += 2 * D
        raw = view(at, 2, T + 4); at += 2 * (T + 4)
        cond = view(at, 2, KT, 2); at += 4 * KT
        modrow = view(at, 2, 512); at += 1024
        junk = htmp
        kcache, vcache = view(at, P), view(at + P, P); at += 2 * P

        chunk_src = [(w_mod[0][:, 512 * j:512 * (j + 1)], 512) for j in range(4)]
        for lo, hi in ((0, 512), (512, 768), (768, 1280), (1280, 1792), (1792, 2304), (2304, 2528)):
            chunk_src.append((w_in[0][:, lo:hi], hi - lo))

        ld_const, ld_x, ld_small, ld_ring0, ld_ring1, ld_ring2 = (
            sem(n) for n in ("ld_const", "ld_x", "ld_small", "ld_ring0", "ld_ring1", "ld_ring2"))
        ld_ring = [ld_ring0, ld_ring1, ld_ring2]
        ring_used, lora_zero, cond_ready, cond_sig = sem("ring_used"), sem("lora_zero"), sem("cond_ready"), sem("cond_sig")
        mu_ready = sem("mu_ready")
        modrow_mm, modrow_ok, bc_mm, bc_ok = sem("modrow_mm"), sem("modrow_ok"), sem("bc_mm"), sem("bc_ok")
        ld_bg = sem("ld_bg")
        ssq_ok, var_ok, std_ok, h_ok, hT_mm, hT_ok = (sem(n) for n in ("ssq_ok", "var_ok", "std_ok", "h_ok", "hT_mm", "hT_ok"))
        qkv_mm, q_ok, kv_ok, rw_mm, raw_ok, shift_ok = (sem(n) for n in ("qkv_mm", "q_ok", "kv_ok", "rw_mm", "raw_ok", "shift_ok"))
        st_cv, raw_zero = sem("st_cv"), sem("raw_zero")
        dve1, act1, pool1 = sem("dve1"), sem("act1"), sem("pool1")
        bmod2 = view(CB + NET * T, 4, 512)
        g1row = view(CB + NET * T + 2048, D)
        assert at <= 53000, at

        def col(v):
            return v.rearrange("(t p) -> p t", p=P)

        small = [
            (mu[:, 0, 0:13], col(mu_shift[0, 0, 0:13 * P])), (mu[:, 1, 0:13], col(mu_shift[0, 1, 0:13 * P])),
            (mu[0:96, 0, 13:14], mu_shift[0, 0, 13 * P:].rearrange("(p a) -> p a", a=1)),
            (mu[0:96, 1, 13:14], mu_shift[0, 1, 13 * P:].rearrange("(p a) -> p a", a=1)),
            (kkv, col(k_k[0])), (kav, col(k_a[0])), (rkv, col(r_k[0].rearrange("h k -> (h k)"))),
            (lngv, col(ln_x_g[0])), (lnbv, col(ln_x_b[0])),
            (gq, q_norm_g[0].partition_broadcast(P)), (gk, k_norm_g[0].partition_broadcast(P)),
            (glora[0:GATE_LORA, :], g_lora_up[0]),
            (router[:, :, 0:NG], router_c[0].rearrange("(k p) n -> p k n", p=P)),
            (router[:, :, NG:], router_f[0].rearrange("(k p) n -> p k n", p=P)),
            (rbias[:, 0:NG], router_c_b[0].partition_broadcast(P)),
            (rbias[:, NG:], router_f_b[0].partition_broadcast(P)),
            (kcache, cache_k[0, 0].rearrange("s h d -> s (h d)")),
            (vcache, cache_v[0, 0].rearrange("s h d -> s (h d)")),
        ]
        for z in range(2):
            small += [(w0v[:, z, :], col(w0[0, z])), (a0v[:, z, :], col(a0[0, z]))]

        with nc.Block() as block:
            @block.sync
            def _(sp):
                for n, (src, w) in enumerate(chunk_src):
                    if n >= 3:
                        sp.wait_ge(ring_used, n - 2)
                    sp.dma_start(ring[:, n % 3, :, 0:w], src.rearrange("(k p) n -> p k n", p=P)).then_inc(ld_ring[n % 3], 16)
                    if n == 1:
                        for tt in range(NTT):
                            src_x = x_prompt[0] if tt == 0 else x_sample[0, (tt - 1) * P:tt * P, :]
                            sp.dma_start(xs[:, tt, :], src_x).then_inc(ld_x, 16)
                sp.wait_ge(shift_ok, NET)
                sp.wait_ge(kv_ok, NTT)
                sp.dma_start(new_cache_v[0, 0].rearrange("s h d -> s (h d)"), qkv[:, 0, D_ATTN + D_KV:]).then_inc(st_cv, 16)
                sp.wait_ge(st_cv, 16)

            @block.gpsimd
            def _(pool):
                pool.memset(lorabd, 0.0).then_inc(lora_zero, 1)
                pool.memset(raw, 0.0).then_inc(raw_zero, 1)

            @block.scalar
            def _(act):
                for i, v in enumerate((c_ctx, c[0])):
                    act.dma_start(cond[:, 0, :, i], v.rearrange("(k p) -> p k", p=P), allow_slow_non_contiguous=True).then_inc(ld_bg, 16)
                act.dma_start(const, consts).then_inc(ld_const, 16)
                for j in range(4):
                    act.dma_start(bmod2[0:2, j, :], b_mod[0, 512 * j:512 * (j + 1)].partition_broadcast(2)).then_inc(ld_bg, 16)
                act.dma_start(g1row[0:2, :], norm1_g[0].partition_broadcast(2)).then_inc(ld_bg, 16)
                for dst, src in small:
                    act.dma_start(dst, src, allow_slow_non_contiguous=True).then_inc(ld_small, 16)
                act.wait_ge(lora_zero, 1)
                for z in range(2):
                    act.dma_start(lorabd[32 * z:32 * z + 32, z, :], w_lora_up[0, z]).then_inc(ld_small, 16)
                    act.dma_start(lorabd[64 + 32 * z:96 + 32 * z, 2 + z, :], a_lora_up[0, z]).then_inc(ld_small, 16)
                act.wait_ge(ld_bg, 16 * 7)
                act.activation(cond[:, 1], cond[:, 0], ACT.Sigmoid).then_inc(cond_sig, 1)
                act.wait_ge(ld_x, 16 * NTT)
                ch = Chain(act, act1)
                for tt in range(NTT):
                    ch(act.activation(junk[:, tt % 2, :], xs[:, tt, :], ACT.Square, accum_out=ssq[:, tt:tt + 1]))
                act.wait_ge(var_ok, 1)
                act.activation(rstd, ssq, ACT.Sqrt).then_inc(std_ok, 1)
                n = 0
                for j in range(4):
                    for cc in range(2):
                        act.wait_ge(bc_mm, n + 1)
                        dst = (shift1 if j < 2 else gain1)[:, cc, 512 * (j % 2):512 * (j % 2 + 1)]
                        act.activation(dst, ps[:, 4 + n % 4, :], ACT.Copy).then_inc(bc_ok, 1)
                        n += 1
                for tt in range(NTT):
                    act.wait_ge(hT_mm, tt + 1)
                    b = 2 * (tt % 2)
                    act.activation(hT[:, :, tt * P:(tt + 1) * P],
                                   ps[:, b:b + 2, :].rearrange("p b (k t) -> p (b k) t", t=P), ACT.Copy).then_inc(hT_ok, 1)
                for tt in range(NTT):
                    act.wait_ge(qkv_mm, 2 * tt + 1)
                    act.activation(qkv[:, tt, 0:512], ps[:, 4 + 2 * (tt % 2), :], ACT.Copy).then_inc(q_ok, 1)
                act.wait_ge(ld_small, 16 * (len(small) + 4))
                act.wait_ge(raw_zero, 1)
                for e in range(NET):
                    m = P if e < NET - 1 else GATE_LORA
                    act.wait_ge(rw_mm, e + 1)
                    if e >= 2:
                        act.wait_ge(shift_ok, e - 1)
                    if e == 0:
                        act.wait_ge(mu_ready, 1)
                    act.activation(raw[0:m, e % 2, 1:129], ps[0:m, 2 + e % 2, 0:T_CTX], ACT.Copy)
                    act.activation(raw[0:m, e % 2, 130:642], ps[0:m, e % 2, :], ACT.Copy)
                    act.activation(rws[0:m, e, 0:T_CTX], ps[0:m, 2 + e % 2, 0:T_CTX], ACT.Copy, scale=mu_c0[0:m, e:e + 1])
                    act.activation(rws[0:m, e, T_CTX:], ps[0:m, e % 2, :], ACT.Copy, scale=mu_c0[0:m, e:e + 1]).then_inc(raw_ok, 1)

            @block.vector
            def _(dve):
                ch = Chain(dve, dve1)
                dve.wait_ge(ld_small, 16 * (len(small) + 4))
                ch(dve.memset(mu_c0, 1.0))
                for z in range(2):
                    for m, lo, hi in ((P, 0, NET - 1), (GATE_LORA, NET - 1, NET)):
                        ins = dve.tensor_tensor(mu_c0[0:m, lo:hi], mu_c0[0:m, lo:hi], mu[0:m, z, lo:hi], ALU.subtract)
                        ch(ins) if z == 0 or lo == 0 else ins.then_inc(mu_ready, 1)
                ch(dve.tensor_scalar(ka1v, kav, -1.0, 1.0, ALU.mult, ALU.add))
                dve.wait_ge(cond_sig, 1)
                dve.tensor_tensor(cond2, cond[:, 1], cond[:, 0], ALU.mult).then_inc(cond_ready, 1)
                dve.wait_ge(act1, NTT)
                dve.tensor_scalar(ssq, ssq, 1.0 / D, EPS, ALU.mult, ALU.add).then_inc(var_ok, 1)
                dve.wait_ge(std_ok, 1)
                ch(dve.reciprocal(rstd, rstd))
                dve.wait_ge(ld_bg, 16 * 7)
                for j in range(4):
                    dve.wait_ge(modrow_mm, j + 1)
                    row = modrow[0:2, j % 2, :]
                    if j >= 2:
                        dve.wait_ge(bc_mm, 2 * (j - 1))
                    if j < 2:
                        dve.tensor_tensor(row, ps[0:2, j, :], bmod2[0:2, j, :], ALU.add).then_inc(modrow_ok, 1)
                    else:
                        ch(dve.tensor_tensor(row, ps[0:2, j, :], bmod2[0:2, j, :], ALU.add))
                        dve.scalar_tensor_tensor(row, row, 1.0, g1row[0:2, 512 * (j - 2):512 * (j - 1)],
                                                 ALU.add, ALU.mult).then_inc(modrow_ok, 1)
                dve.wait_ge(bc_ok, 8)
                for tt in range(NTT):
                    cc = 0 if tt == 0 else 1
                    if tt >= 2:
                        dve.wait_ge(hT_mm, tt - 1)
                    ch(dve.scalar_tensor_tensor(htmp[:, tt % 2, :], xs[:, tt, :], rstd[:, tt:tt + 1], gain1[:, cc, :],
                                                ALU.mult, ALU.mult))
                    dve.tensor_tensor(htmp[:, tt % 2, :], htmp[:, tt % 2, :], shift1[:, cc, :], ALU.add).then_inc(h_ok, 1)
                for tt in range(NTT):
                    dve.wait_ge(qkv_mm, 2 * tt + 2)
                    dve.tensor_copy(qkv[:, tt, 512:768], ps[:, 5 + 2 * (tt % 2), 0:256]).then_inc(kv_ok, 1)
                for e in range(NET):
                    m = P if e < NET - 1 else GATE_LORA
                    dve.wait_ge(raw_ok, e + 1)
                    r_, o = raw[0:m, e % 2, :], rws[0:m, e, :]
                    for k, off in ((0, 0), (1, 2)):
                        for (a, b), base in (((0, T_CTX), 0), ((T_CTX, T), T_CTX + 1)):
                            ins = dve.scalar_tensor_tensor(o[:, a:b], r_[:, base + off:base + off + b - a],
                                                           mu[0:m, k, e:e + 1], o[:, a:b], ALU.mult, ALU.add)
                            if k == 1 and a:
                                ins.then_inc(shift_ok, 1)
                            else:
                                ch(ins)

            @block.tensor
            def _(pe):
                pe.wait_ge(cond_ready, 1)
                for j in range(4):
                    pe.wait_ge(ld_ring[j % 3], 16 * (j // 3 + 1))
                    for k in range(KT):
                        mm = pe.matmul(ps[0:2, j, :], cond2[:, k, :], ring[:, j % 3, k, :], start=(k == 0), stop=(k == KT - 1))
                    mm.then_inc(modrow_mm, 1)
                    pe.wait_ge(modrow_mm, j + 1)
                    pe.nop().then_inc(ring_used, 1)
                pe.wait_ge(ld_const, 16)
                n = 0
                for j in range(4):
                    pe.wait_ge(modrow_ok, j + 1)
                    for cc in range(2):
                        if n >= 4:
                            pe.wait_ge(bc_ok, n - 3)
                        pe.matmul(ps[:, 4 + n % 4, :], sel[0:2, cc, :], modrow[0:2, j % 2, :], start=True, stop=True).then_inc(bc_mm, 1)
                        n += 1
                for tt in range(NTT):
                    pe.wait_ge(h_ok, tt + 1)
                    if tt >= 2:
                        pe.wait_ge(hT_ok, tt - 1)
                    b = 2 * (tt % 2)
                    for k in range(KT):
                        mm = pe.transpose(ps[:, b + k // 4, (k % 4) * P:(k % 4 + 1) * P], htmp[:, tt % 2, k * P:(k + 1) * P], ident)
                    mm.then_inc(hT_mm, 1)
                pe.wait_ge(hT_ok, NTT)
                pe.wait_ge(bc_ok, 8)
                pe.wait_ge(ld_ring[1], 32)
                pe.wait_ge(ld_ring[2], 32)
                for tt in range(NTT):
                    b = 4 + 2 * (tt % 2)
                    if tt >= 2:
                        pe.wait_ge(q_ok, tt - 1)
                        pe.wait_ge(kv_ok, tt - 1)
                    for half, w in ((0, 512), (1, 256)):
                        for k in range(KT):
                            mm = pe.matmul(ps[:, b + half, 0:w], hT[:, k, tt * P:(tt + 1) * P],
                                           ring[:, (4 + half) % 3, k, 0:w], start=(k == 0), stop=(k == KT - 1))
                        mm.then_inc(qkv_mm, 1)
                pe.wait_ge(qkv_mm, 2 * NTT)
                pe.nop().then_inc(ring_used, 1)
                pe.nop().then_inc(ring_used, 1)
                for e in range(NET):
                    n = 6 + e // 4
                    if e % 4 == 0:
                        pe.wait_ge(ld_ring[n % 3], 16 * (n // 3 + 1))
                    m = P if e < NET - 1 else GATE_LORA
                    if e >= 2:
                        pe.wait_ge(raw_ok, e - 1)
                    for lo, hi, b in ((T_CTX, T, e % 2), (0, T_CTX, 2 + e % 2)):
                        for k in range(KT):
                            mm = pe.matmul(ps[0:m, b, 0:hi - lo], ring[:, n % 3, k, (e % 4) * P:(e % 4) * P + m],
                                           hT[:, k, lo:hi], start=(k == 0), stop=(k == KT - 1))
                    mm.then_inc(rw_mm, 1)
                    if e % 4 == 3:
                        pe.wait_ge(rw_mm, e + 1)
                        pe.nop().then_inc(ring_used, 1)

        at = R
        sq = view(at, NTT, 640)
        qn = view(at + 3200, NTT, 640); at += 6400
        qT = view(at, 4, T); at += 4 * T
        kT = view(at, T + PAST); at += T + PAST
        prob = view(at, 2, 640); at += 1280
        probT = view(at, 2, 640); at += 1280
        rot1 = view(at, 640); rot2 = view(at + 640, 640); at += 1280
        attn = view(at, NTT, 512); at += NTT * 512
        attnT = view(at, 4, T); at += 4 * T
        hss, hrs = view(at, NTT, 10), view(at + 50, NTT, 10); at += 100
        negmax, rsum, rinv = view(at, 40), view(at + 40, 40), view(at + 80, 40); at += 120
        zrow = view(at, D); at += D
        SC = HD ** -0.5

        z_set, z_filled = sem("z_set"), sem("z_filled")
        units = [(tt, h) for tt in range(NTT) for h in range(NQ)]
        (sq_ok, hss_ok, hstd_ok, qn_ok, kc_out, tp_mm, tp_ok, s_mm, max_ok, exp_ok, pt_mm, pt_ok, pv_mm, at_ok,
         aT_mm, aT_ok, st_aT, dve2, act2) = (sem(n) for n in (
             "sq_ok", "hss_ok", "hstd_ok", "qn_ok", "kc_out", "tp_mm", "tp_ok", "s_mm", "max_ok", "exp_ok", "pt_mm",
             "pt_ok", "pv_mm", "at_ok", "aT_mm", "aT_ok", "st_aT", "dve2", "act2"))

        with nc.Block() as block:
            @block.sync
            def _(sp):
                sp.wait_ge(z_set, 1)
                sp.dma_start(xg_d.rearrange("(n p) d -> p n d", p=P), zrow.unsqueeze(1).to_broadcast([P, NT + 1, D])).then_inc(z_filled, 16)
                sp.wait_ge(qn_ok, 1)
                sp.dma_start(new_cache_k[0, 0].rearrange("s h d -> s (h d)"), qn[:, 0, 512:640]).then_inc(kc_out, 16)
                sp.wait_ge(aT_ok, NTT)
                sp.dma_start(attn_d, attnT.rearrange("p a t -> p (a t)")).then_inc(st_aT, 16)
                sp.wait_ge(kc_out, 16)
                sp.wait_ge(st_aT, 16)
                sp.wait_ge(z_filled, 16)

            @block.gpsimd
            def _(pool):
                pool.memset(zrow, 0.0).then_inc(z_set, 1)

            @block.vector
            def _(dve):
                ch = Chain(dve, dve2)
                dve.wait_ge(sq_ok, 1)
                ch(dve.tensor_reduce(hss.rearrange("p a b -> p (a b)"), sq.rearrange("p a (h d) -> p (a h) d", d=HD), AX.X, ALU.add))
                dve.tensor_scalar(hss, hss, 1.0 / HD, EPS, ALU.mult, ALU.add).then_inc(hss_ok, 1)
                dve.wait_ge(hstd_ok, 1)
                ch(dve.reciprocal(hrs, hrs))
                for tt in range(NTT):
                    x = qn[:, tt, :]
                    xh = x.rearrange("p (h d) -> p h d", d=HD)
                    q_out = x[:, 0:512].rearrange("p (j g d) -> p g j d", g=2, d=HD)
                    r1 = rot1.rearrange("p (h d) -> p h d", d=HD)
                    ch(dve.tensor_tensor(r1, qkv[:, tt, 0:640].rearrange("p (h d) -> p h d", d=HD),
                                         hrs[:, tt, :].unsqueeze(2).to_broadcast([P, 10, HD]), ALU.mult))
                    if tt == 0:
                        for g in range(2):
                            dve.tensor_tensor(q_out[:, g], r1[:, 4 * g:4 * g + 4], gq.unsqueeze(1).to_broadcast([P, 4, HD]), ALU.mult)
                        dve.tensor_tensor(xh[:, 8:10], r1[:, 8:10], gk.unsqueeze(1).to_broadcast([P, 2, HD]), ALU.mult).then_inc(qn_ok, 1)
                        dve.wait_ge(qn_ok, 1)
                        continue
                    dve.tensor_tensor(xh[:, 0:8], r1[:, 0:8], gq.unsqueeze(1).to_broadcast([P, 8, HD]), ALU.mult)
                    ch(dve.tensor_tensor(xh[:, 8:10], r1[:, 8:10], gk.unsqueeze(1).to_broadcast([P, 2, HD]), ALU.mult))
                    cosb = rope_c[:, tt - 1, :].unsqueeze(1).to_broadcast([P, 10, HD])
                    dve.tensor_tensor(r1, xh, cosb, ALU.mult)
                    x4 = x.rearrange("p (h a d) -> p h a d", a=4, d=16)
                    o4 = rot2.rearrange("p (h a d) -> p h a d", a=4, d=16)
                    s4 = rope_s[:, tt - 1, :].rearrange("p (a d) -> p a d", a=4)
                    for k in range(4):
                        ins = dve.tensor_tensor(o4[:, :, k, :], x4[:, :, k ^ 1, :],
                                                s4[:, k, :].unsqueeze(1).to_broadcast([P, 10, 16]), ALU.mult)
                    ch(ins)
                    r2 = rot2.rearrange("p (h d) -> p h d", d=HD)
                    for g in range(2):
                        dve.tensor_tensor(q_out[:, g], r1[:, 4 * g:4 * g + 4], r2[:, 4 * g:4 * g + 4], ALU.add)
                    dve.tensor_tensor(xh[:, 8:10], r1[:, 8:10], r2[:, 8:10], ALU.add).then_inc(qn_ok, 1)
                    dve.wait_ge(qn_ok, tt + 1)
                for n, (tt, h) in enumerate(units + [(0, 0)] * 2):
                    if n < len(units):
                        w = P if tt == 0 else 640
                        dve.wait_ge(s_mm, n + 1)
                        s_ = ps[:, 2 * (n % 2):2 * (n % 2) + 2, :].rearrange("p b n -> p (b n)")[:, 0:w]
                        ch(dve.reduce_max(negmax[:, n:n + 1], s_, AX.X))
                        dve.tensor_scalar(negmax[:, n:n + 1], negmax[:, n:n + 1], -SC, None, ALU.mult).then_inc(max_ok, 1)
                    if n >= 2:
                        m = n - 2
                        ch(dve.reciprocal(rinv[:, m:m + 1], rsum[:, m:m + 1]))
                        dve.wait_ge(pv_mm, m + 1)
                        tm, hm = units[m]
                        dve.tensor_scalar(attn[:, tm, hm * HD:(hm + 1) * HD], ps[:, 6 + m % 2, 0:HD], rinv[:, m:m + 1],
                                          None, ALU.mult).then_inc(at_ok, 1)

            @block.scalar
            def _(act):
                act.activation(sq, qkv[:, :, 0:640], ACT.Square).then_inc(sq_ok, 1)
                act.wait_ge(hss_ok, 1)
                act.activation(hrs, hss, ACT.Sqrt).then_inc(hstd_ok, 1)
                act.wait_ge(tp_mm, 1)
                act.activation(kT[:, T:T + PAST], ps[:, 0, 0:P], ACT.Copy).then_inc(tp_ok, 1)
                for tt in range(NTT):
                    act.wait_ge(tp_mm, tt + 2)
                    b = 2 * ((tt + 1) % 2)
                    act.activation(kT[:, tt * P:(tt + 1) * P], ps[:, b, 0:P], ACT.Copy)
                    act.activation(qT[:, :, tt * P:(tt + 1) * P], ps[:, b + 1, :].rearrange("p (j t) -> p j t", t=P),
                                   ACT.Copy).then_inc(tp_ok, 1)
                for n, (tt, h) in enumerate(units + [(0, 0)]):
                    if n < len(units):
                        w = P if tt == 0 else 640
                        act.wait_ge(max_ok, n + 1)
                        if n >= 2:
                            act.wait_ge(pt_mm, n - 1)
                        s_ = ps[:, 2 * (n % 2):2 * (n % 2) + 2, :].rearrange("p b n -> p (b n)")[:, 0:w]
                        act.activation(prob[:, n % 2, 0:w], s_, ACT.Exp, bias=negmax[:, n:n + 1], scale=SC,
                                       accum_out=rsum[:, n:n + 1]).then_inc(exp_ok, 1)
                    if n >= 1:
                        m = n - 1
                        wm = P if units[m][0] == 0 else 640
                        act.wait_ge(pt_mm, m + 1)
                        if m >= 2:
                            act.wait_ge(pv_mm, m - 1)
                        act.activation(probT[:, m % 2, 0:wm],
                                       ps[:, 4:6, :].rearrange("p b n -> p (b n)")[:, 0:wm], ACT.Copy).then_inc(pt_ok, 1)
                for tt in range(NTT):
                    act.wait_ge(aT_mm, tt + 1)
                    act.activation(attnT[:, :, tt * P:(tt + 1) * P], ps[:, tt % 2, :].rearrange("p (j t) -> p j t", t=P),
                                   ACT.Copy).then_inc(aT_ok, 1)

            @block.tensor
            def _(pe):
                pe.transpose(ps[:, 0, 0:P], kcache, ident).then_inc(tp_mm, 1)
                for tt in range(NTT):
                    pe.wait_ge(qn_ok, tt + 1)
                    if tt >= 1:
                        pe.wait_ge(tp_ok, tt)
                    b = 2 * ((tt + 1) % 2)
                    pe.transpose(ps[:, b, 0:P], qn[:, tt, 512:640], ident)
                    for j in range(4):
                        mm = pe.transpose(ps[:, b + 1, j * P:(j + 1) * P],
                                          qn[:, tt, j * P:(j + 1) * P], ident)
                    mm.then_inc(tp_mm, 1)
                pe.wait_ge(tp_ok, NTT + 1)

                def scores(n):
                    tt, h = units[n]
                    if n >= 2:
                        pe.wait_ge(exp_ok, n - 1)
                    r = slice(64 * (h // 4), 64 * (h // 4) + 64)
                    q_ = qT[r, h % 4, tt * P:(tt + 1) * P]
                    b = 2 * (n % 2)
                    if tt == 0:
                        mm = pe.matmul(ps[:, b, 0:P], q_, kT[r, 0:P], start=True, stop=True)
                    else:
                        pe.matmul(ps[:, b, :], q_, kT[r, P:T], start=True, stop=True)
                        mm = pe.matmul(ps[:, b + 1, 0:P], q_, kT[r, T:T + PAST], start=True, stop=True)
                    mm.then_inc(s_mm, 1)

                def transposes(n):
                    tt, h = units[n]
                    pe.wait_ge(exp_ok, n + 1)
                    if n >= 1:
                        pe.wait_ge(pt_ok, n)
                    for y in range(1 if tt == 0 else 5):
                        mm = pe.transpose(ps[:, 4 + y // 4, (y % 4) * P:(y % 4 + 1) * P], prob[:, n % 2, y * P:(y + 1) * P], ident)
                    mm.then_inc(pt_mm, 1)

                def values(n):
                    tt, h = units[n]
                    pe.wait_ge(pt_ok, n + 1)
                    if n >= 2:
                        pe.wait_ge(at_ok, n - 1)
                    v0 = D_ATTN + D_KV + HD * (h // 4)
                    if tt == 0:
                        vs = [qkv[:, 0, v0:v0 + HD]]
                    else:
                        vs = [qkv[:, y, v0:v0 + HD] for y in range(1, NTT)] + [vcache[:, HD * (h // 4):HD * (h // 4) + HD]]
                    for y, v_ in enumerate(vs):
                        mm = pe.matmul(ps[:, 6 + n % 2, 0:HD], probT[:, n % 2, y * P:(y + 1) * P], v_,
                                       start=(y == 0), stop=(y == len(vs) - 1))
                    mm.then_inc(pv_mm, 1)

                scores(0)
                for n in range(len(units)):
                    if n + 1 < len(units):
                        scores(n + 1)
                    transposes(n)
                    if n >= 1:
                        values(n - 1)
                values(len(units) - 1)
                for tt in range(NTT):
                    pe.wait_ge(at_ok, min(len(units), NQ * (tt + 1)))
                    if tt >= 2:
                        pe.wait_ge(aT_ok, tt - 1)
                    for j in range(4):
                        mm = pe.transpose(ps[:, tt % 2, j * P:(j + 1) * P], attn[:, tt, j * P:(j + 1) * P], ident)
                    mm.then_inc(aT_mm, 1)

        chm = view(R, 2, 4, NC4, T)
        bonus = view(R + 8 * NC4 * T, NC4, T)
        at = R + 9 * NC4 * T
        t_cs, t_csm, t_e, t_em, t_ei, t_kd, t_b, t_x, t_rk = (view(at + i * T, T) for i in range(9)); at += 9 * T
        ksq = view(at, NC4, T)
        assert at + NC4 * T <= 53000, at
        A_, R_, B_, K_ = range(4)
        lora_in, gate_in = rws[:, 12, :], rws[:, 13, :]
        (lact_ok, wl_mm, sig_ok, kk_ok, ksq_ok, n_mm, n_ok, nstd_ok, rk_ok, bo_mm, bo_ok, cs_ok, csm_ok, exps_ok,
         ops_done, st_bo, dve3, act3) = (sem(n) for n in (
             "lact_ok", "wl_mm", "sig_ok", "kk_ok", "ksq_ok", "n_mm", "n_ok", "nstd_ok", "rk_ok", "bo_mm", "bo_ok",
             "cs_ok", "csm_ok", "exps_ok", "ops_done", "st_bo", "dve3", "act3"))

        def two_banks(b, m=P):
            return ps[0:m, b:b + 2, 0:T // 2]

        def halves(v):
            return v.rearrange("p (b n) -> p b n", b=2)

        with nc.Block() as block:
            @block.sync
            def _(sp):
                sp.wait_ge(bo_ok, NC4)
                sp.dma_start(bonus_d, bonus.rearrange("p a t -> p (a t)")).then_inc(st_bo, 16)
                sp.wait_ge(st_bo, 16)

            @block.tensor
            def _(pe):
                pe.wait_ge(lact_ok, 1)
                n = 0
                for c4 in range(NC4):
                    for j in range(4):
                        if n >= 2:
                            pe.wait_ge(sig_ok, n - 1)
                        for hf in range(2):
                            mm = pe.matmul(ps[:, 2 * (n % 2) + hf, 0:T // 2], lorabd[:, j, c4 * P:(c4 + 1) * P],
                                           lora_in[:, hf * T // 2:(hf + 1) * T // 2], start=True, stop=True)
                        mm.then_inc(wl_mm, 1)
                        n += 1
                for c4 in range(NC4):
                    pe.wait_ge(ksq_ok, c4 + 1)
                    if c4 >= 1:
                        pe.wait_ge(n_ok, c4)
                    for hf in range(2):
                        mm = pe.matmul(ps[:, 4 + hf, 0:T // 2], blockones, ksq[:, c4, hf * T // 2:(hf + 1) * T // 2], start=True, stop=True)
                    mm.then_inc(n_mm, 1)
                    pe.wait_ge(rk_ok, c4 + 1)
                    if c4 >= 1:
                        pe.wait_ge(bo_ok, c4)
                    for hf in range(2):
                        mm = pe.matmul(ps[:, 6 + hf, 0:T // 2], blockones, t_rk[:, hf * T // 2:(hf + 1) * T // 2], start=True, stop=True)
                    mm.then_inc(bo_mm, 1)

            @block.scalar
            def _(act):
                ch = Chain(act, act3)
                ch(act.activation(gate_in[0:GATE_LORA, :], gate_in[0:GATE_LORA, :], ACT.Sigmoid))
                act.activation(lora_in[0:64, :], lora_in[0:64, :], ACT.Tanh).then_inc(lact_ok, 1)
                n = 0
                for c4 in range(NC4):
                    for j in range(4):
                        act.wait_ge(wl_mm, n + 1)
                        dst = chm[:, j % 2, B_ if j < 2 else K_, c4, :]
                        bias = (w0v if j < 2 else a0v)[:, j % 2, c4:c4 + 1]
                        act.activation(halves(dst), two_banks(2 * (n % 2)), ACT.Sigmoid, bias=bias).then_inc(sig_ok, 1)
                        n += 1
                act.wait_ge(n_ok, NC4)
                act.activation(ksq, ksq, ACT.Sqrt).then_inc(nstd_ok, 1)
                n = 0
                for c4 in range(NC4):
                    for z in (1, 0):
                        act.wait_ge(csm_ok, n + 1)
                        act.activation(t_e, t_cs, ACT.Exp, scale=-DS)
                        act.activation(t_em, t_csm, ACT.Exp, scale=-DS)
                        act.activation(t_ei, t_cs, ACT.Exp, scale=DS)
                        last = C - 1 if z == 0 else 0
                        act.activation(pc_all[:, z, c4, :], t_cs.rearrange("p (c t) -> p c t", t=C)[:, :, last],
                                       ACT.Exp, scale=-DS).then_inc(exps_ok, 1)
                        n += 1

            @block.vector
            def _(dve):
                ch = Chain(dve, dve3)
                for c4 in range(NC4):
                    kk = chm[:, 0, A_, c4, :]
                    ch(dve.tensor_scalar(kk, rws[:, 4 + c4, :], kkv[:, c4:c4 + 1], None, ALU.mult))
                    dve.tensor_tensor(ksq[:, c4, :], kk, kk, ALU.mult).then_inc(ksq_ok, 1)
                    if c4 >= 1:
                        dve.wait_ge(bo_mm, c4)
                    dve.scalar_tensor_tensor(t_rk, rws[:, c4, :], rkv[:, c4:c4 + 1], rws[:, 4 + c4, :], ALU.mult, ALU.mult).then_inc(rk_ok, 1)
                    dve.wait_ge(n_mm, c4 + 1)
                    dve.tensor_scalar(halves(ksq[:, c4, :]), two_banks(4), 1e-12, None, ALU.add).then_inc(n_ok, 1)
                    dve.wait_ge(bo_mm, c4 + 1)
                    dve.tensor_tensor(halves(bonus[:, c4, :]), two_banks(6), halves(rws[:, 8 + c4, :]), ALU.mult).then_inc(bo_ok, 1)
                dve.wait_ge(nstd_ok, 1)
                ch(dve.reciprocal(ksq, ksq))
                ch(dve.tensor_tensor(chm[:, 0, A_], chm[:, 0, A_], ksq, ALU.mult))
                dve.wait_ge(sig_ok, 4 * NC4)
                n = 0
                for c4 in range(NC4):
                    kk, r_, k_ = chm[:, 0, A_, c4, :], rws[:, c4, :], rws[:, 4 + c4, :]
                    for z in (1, 0):
                        sig, rate = chm[:, z, B_, c4, :], chm[:, z, K_, c4, :]
                        if n >= 1:
                            dve.wait_ge(exps_ok, n)
                        if z == 0:
                            ch(dve.tensor_tensor_scan(t_cs, scanmask, sig, 0.0, ALU.mult, ALU.add))
                        else:
                            ch(dve.tensor_tensor_scan(t_x, scanmask, sig, 0.0, ALU.mult, ALU.add))
                            x3 = t_x.rearrange("p (c t) -> p c t", t=C)
                            ch(dve.tensor_tensor(t_cs.rearrange("p (c t) -> p c t", t=C),
                                                 x3[:, :, C - 1:C].to_broadcast([P, NCH, C]), x3, ALU.subtract))
                            ch(dve.tensor_tensor(t_cs, t_cs, sig, ALU.add))
                        dve.tensor_tensor(t_csm, t_cs, sig, ALU.subtract).then_inc(csm_ok, 1)
                        dve.tensor_tensor(t_b, kk, rate, ALU.mult)
                        ch(dve.tensor_scalar(t_kd, rate, kav[:, c4:c4 + 1], ka1v[:, c4:c4 + 1], ALU.mult, ALU.add))
                        ch(dve.tensor_tensor(t_kd, t_kd, k_, ALU.mult))
                        dve.wait_ge(exps_ok, n + 1)
                        dve.tensor_tensor(chm[:, z, B_, c4, :], t_b, t_ei, ALU.mult)
                        dve.tensor_tensor(chm[:, z, K_, c4, :], t_kd, t_ei, ALU.mult)
                        dve.tensor_tensor(chm[:, z, R_, c4, :], r_, t_e, ALU.mult)
                        ch(dve.tensor_tensor(chm[:, z, A_, c4, :], kk, t_em, ALU.mult))
                        n += 1

        with nc.Block() as block:
            @block.gpsimd
            def _(pool):
                nc.clear_and_free_semaphores(phase_sems)

        BDC = NC4 * P
        bdin = view(CB, 2, 5, NC4, P)
        at = CB + NET * T
        yacc = view(at, NCH, NC4, C); at += NCH * NC4 * C
        S = view(at, 2, NC4, C); at += 2 * NC4 * C
        Vc = view(at, 2, NC4, C); at += 2 * NC4 * C
        assert at <= R
        at = R + 8 * NC4 * T
        LTb = view(at, 2, NC4, P); at += 2 * BDC
        Lm = view(at, 2, 2, NC4, P)
        stage_in = view(at, 2, NC4, C)
        stage_out = view(at + 512, 2, NC4, C)
        at += 4 * BDC
        bdout0 = at
        MTb, RKb, RBb, Ktb, Btb = (view(at + i * 2 * BDC, 2, NC4, P) for i in range(5)); at += 10 * BDC
        Zb, XTb = view(at, 2, NC4, P), view(at + 2 * BDC, 2, NC4, P); at += 4 * BDC
        bdout1 = at
        Xc, XTc, Zc = (view(at + i * 2 * NC4 * C, 2, NC4, C) for i in range(3)); at += 6 * NC4 * C
        RHc, Uc = Zc, XTc
        assert at <= 53000, at
        N_CTX = T_CTX // C
        spans = ((0, N_CTX, 0), (T_CTX, T_LAT // C, N_CTX))

        def sems(*names):
            return [[sem(f"{n}_{d}") for d in ("fwd", "bwd")] for n in names]

        (bdg, bds, lm_ok, gB, gK, gT, w_mm, xt_mm, xq_mm, rhs_mm, u_mm, y_mm, sn_mm, lt_ok, rb_ok, rk_ok, tr_ok, z_ok,
         xt_ok, xc_ok, rh_ok, uc_ok, y_ok, s_add, s_ok) = sems(
            "bd_bkv", "bd_ar", "lm_ok", "gram_b", "gram_k", "gram_t", "w_mm", "xt_mm", "xq_mm", "rhs_mm", "u_mm",
            "y_mm", "sn_mm", "lt_ok", "rb_ok", "rk_ok", "tr_ok", "z_ok", "xt_ok", "xc_ok", "rh_ok", "uc_ok", "y_ok",
            "s_add", "s_ok")
        zero4, half_ok, ld_state, st_state, so_mm, si_mm, so_ok, si_ok = (sem(n) for n in (
            "zero4", "half_ok", "ld_state", "st_state", "state_out_mm", "state_in_mm", "state_out_ok", "state_in_ok"))
        GB, GK, GT, GV = 0, 1, 2, 3

        def start_counts(eng, *pairs):
            for pair in pairs:
                for one in pair:
                    eng.nop().then_inc(one, 1)

        def quarter(bank, first=0):
            return ps[:, bank, first:first + NC4 * C].rearrange("p (j n) -> p j n", j=NC4)

        def diag(v, p):
            return v[64 * p:64 * p + 64, :, 64 * p:64 * p + 64]

        def rows(v, p):
            return v[64 * p:64 * p + 64]

        def chunks(eng, i, t0, n, size=C):
            f = t0 // C
            return eng.snap((i + f) * size), eng.snap((i * -1 + (f + n - 1)) * size)

        with nc.Block() as block:
            @block.sync
            def _(sp):
                sp.wait_ge(so_mm, 1)
                for z in range(2):
                    for p in range(2):
                        sp.dma_start(rows(stage_in[:, z], p), state_rwkv[0, 0, z].rearrange("(j p) v k -> p v j k", p=2)[p]).then_inc(ld_state, 16)
                sp.wait_ge(so_ok, 1)
                for z in range(2):
                    for p in range(2):
                        sp.dma_start(new_state[0, 0, z].rearrange("(j p) v k -> p v j k", p=2)[p], rows(stage_out[:, z], p)).then_inc(st_state, 16)
                sp.wait_ge(st_state, 64)

            @block.gpsimd
            def _(pool):
                pool.memset(view(CB, 10 * BDC), 0.0).then_inc(zero4, 1)
                pool.memset(LTb, 0.0).then_inc(zero4, 1)
                pool.memset(view(bdout0, bdout1 - bdout0), 0.0).then_inc(zero4, 1)
                pool.memset(S, 0.0).then_inc(zero4, 1)
                pool.memset(yacc, 0.0).then_inc(zero4, 1)
                pool.wait_ge(zero4, 5)
                start_counts(pool, bdg, bds, lm_ok)
                for t0, n, s0 in spans:
                    if t0:
                        pool.wait_ge(st_state, 64)
                        pool.wait_ge(si_mm, 1)
                    with pool.Fori(0, n) as i:
                        s = i + s0
                        tok = chunks(pool, i, t0, n)
                        for z in range(2):
                            pool.wait_ge(gT[z], s + 1)
                            for p in range(2):
                                r_ = slice(64 * p, 64 * p + 64)
                                pool.tensor_copy(bdin[r_, z, 2:4, :, 64 * p:64 * p + 64].rearrange("p a j t -> p (a j) t"),
                                                 chm[r_, z, 2:4, :, bass.ds(tok[z], C)].rearrange("p a j t -> p (a j) t"))
                                ins = pool.tensor_copy(diag(bdin[:, z, 4], p), rws[r_, 8:12, bass.ds(tok[z], C)])
                                if p == 0:
                                    ins.then_inc(half_ok, 1)
                                    pool.wait_ge(half_ok, s * 4 + z + 1)
                            ins.then_inc(bdg[z], 1)
                            pool.wait_ge(bdg[z], s + 2)

                        def level(z, j):
                            pool.wait_ge(lt_ok[z], s + 2)
                            pool.wait_ge(w_mm[z], s * LEVELS + max(j - 1, 0) + 1)
                            pool.tensor_tensor(Lm[:, z, j % 2], LTb[:, z], levels[:, z, j].unsqueeze(1).to_broadcast([P, NC4, P]),
                                               ALU.mult).then_inc(lm_ok[z], 1)

                        for j in range(2):
                            for z in range(2):
                                level(z, j)
                        pool.wait_ge(lm_ok[1], s * LEVELS + 2 + 1)
                        for z in range(2):
                            pool.wait_ge(y_mm[z], s + 1)
                            for p in range(2):
                                r_ = slice(64 * p, 64 * p + 64)
                                ins = pool.tensor_copy(bdin[r_, z, 0:2, :, 64 * p:64 * p + 64].rearrange("p a j t -> p (a j) t"),
                                                       chm[r_, z, 0:2, :, bass.ds(tok[z], C)].rearrange("p a j t -> p (a j) t"))
                                if p == 0:
                                    ins.then_inc(half_ok, 1)
                                    pool.wait_ge(half_ok, s * 4 + z + 3)
                            ins.then_inc(bds[z], 1)
                            pool.wait_ge(bds[z], s + 2)
                        for j in range(2, LEVELS):
                            for z in range(2):
                                level(z, j)

            @block.tensor
            def _(pe):
                pe.wait_ge(zero4, 5)
                start_counts(pe, gB, gK, gT, w_mm, xt_mm, xq_mm, rhs_mm, u_mm, y_mm, sn_mm)
                for t0, n, s0 in spans:
                    if t0:
                        for z in range(2):
                            pe.wait_ge(s_ok[z], s0 + 1)
                            for p in range(2):
                                for j in range(NC4):
                                    mm = pe.matmul(ps[64 * p:64 * p + 64, 4 + z, j * C:(j + 1) * C], rows(S[:, z, j], p), rows(istack, p), start=True, stop=True)
                        mm.then_inc(so_mm, 1)
                        pe.wait_ge(ld_state, 64)
                        pe.wait_ge(y_ok[0], s0 + 1)
                        pe.wait_ge(y_ok[1], s0 + 1)
                        for z in range(2):
                            for p in range(2):
                                for j in range(NC4):
                                    mm = pe.matmul(ps[64 * p:64 * p + 64, 6 + z, j * C:(j + 1) * C], rows(stage_in[:, z, j], p), rows(istack, p), start=True, stop=True)
                        mm.then_inc(si_mm, 1)
                        pe.wait_ge(so_ok, 1)
                        pe.wait_ge(si_ok, 1)
                    with pe.Fori(0, n) as i:
                        s = i + s0
                        tok = chunks(pe, i, t0, n)
                        for z in range(2):
                            prev = s if z == 0 else s + 1
                            pe.wait_ge(bdg[z], s + 2)
                            ar = [chm[:, z, 0:2, j, bass.ds(tok[z], C)] for j in range(NC4)]
                            pe.wait_ge(rb_ok[1 - z], prev + 1)
                            for j in range(NC4):
                                mm = pe.matmul(ps[:, GB, j * P:(j + 1) * P], bdin[:, z, B_, j], ar[j], start=True, stop=True)
                            mm.then_inc(gB[z], 1)
                            pe.wait_ge(rk_ok[1 - z], prev + 1)
                            for j in range(NC4):
                                mm = pe.matmul(ps[:, GK, j * P:(j + 1) * P], bdin[:, z, K_, j], ar[j], start=True, stop=True)
                            mm.then_inc(gK[z], 1)
                            pe.wait_ge(tr_ok[1 - z], prev + 1)
                            for j in range(NC4):
                                pe.matmul(ps[:, GT, j * C:(j + 1) * C], bdin[:, z, K_, j], istack, start=True, stop=True)
                            for j in range(NC4):
                                pe.matmul(ps[:, GT, 256 + j * C:256 + (j + 1) * C], bdin[:, z, B_, j], istack, start=True, stop=True)
                            for j in range(NC4):
                                mm = pe.matmul(ps[:, GV, j * C:(j + 1) * C], bdin[:, z, 4, j], istack, start=True, stop=True)
                            mm.then_inc(gT[z], 1)
                        for l in range(LEVELS):
                            for z in range(2):
                                pe.wait_ge(lm_ok[z], s * LEVELS + l + 2)
                                if l == 0:
                                    pe.wait_ge(s_ok[z], s + 1)
                                else:
                                    pe.wait_ge(xt_ok[z], s * LEVELS + l + 1)
                                if l >= 2:
                                    pe.wait_ge(xc_ok[z], s * 4 + (l - 1) + 1)
                                for j in range(NC4):
                                    mm = pe.matmul(ps[:, 4 + z, j * C:(j + 1) * C], Lm[:, z, l % 2, j],
                                                   istack if l == 0 else Xc[:, z, j], start=True, stop=True)
                                mm.then_inc(w_mm[z], 1)
                            for z in range(2):
                                pe.wait_ge(z_ok[z], s * LEVELS + l + 2)
                                if 1 <= l < LEVELS - 1:
                                    if l == 1:
                                        pe.wait_ge(y_ok[z], s + 1)
                                    for j in range(NC4):
                                        mm = pe.matmul(ps[:, 6 + z, j * C:(j + 1) * C], XTb[:, z, j], Zc[:, z, j], start=True, stop=True)
                                    mm.then_inc(xq_mm[z], 1)
                                for j in range(NC4):
                                    mm = pe.matmul(ps[:, 4 + z, j * C:(j + 1) * C], Zb[:, z, j],
                                                   istack if l == 0 else XTc[:, z, j], start=True, stop=True)
                                mm.then_inc(xt_mm[z], 1)
                        for z in range(2):
                            pe.wait_ge(bds[z], s + 2)
                            pe.wait_ge(rk_ok[z], s + 2)
                            pe.wait_ge(tr_ok[z], s + 2)
                            pe.wait_ge(xc_ok[z], s * 4 + 4 + 1)
                            for j in range(NC4):
                                pe.matmul(ps[:, 6 + z, j * C:(j + 1) * C], bdin[:, z, A_, j], S[:, z, j], start=True, stop=False)
                                mm = pe.matmul(ps[:, 6 + z, j * C:(j + 1) * C], MTb[:, z, j], Vc[:, z, j], start=False, stop=True)
                            mm.then_inc(rhs_mm[z], 1)
                        for z in range(2):
                            pe.wait_ge(rh_ok[z], s + 2)
                            pe.wait_ge(xt_ok[z], s * LEVELS + LEVELS + 1)
                            for j in range(NC4):
                                mm = pe.matmul(ps[:, 4 + z, j * C:(j + 1) * C], XTb[:, z, j], RHc[:, z, j], start=True, stop=True)
                            mm.then_inc(u_mm[z], 1)
                        for z in range(2):
                            pe.wait_ge(uc_ok[z], s + 2)
                            pe.wait_ge(rb_ok[z], s + 2)
                            for j in range(NC4):
                                out = ps[:, 6 + z, j * C:(j + 1) * C]
                                pe.matmul(out, bdin[:, z, R_, j], S[:, z, j], start=True, stop=False)
                                pe.matmul(out, RKb[:, z, j], Vc[:, z, j], start=False, stop=False)
                                mm = pe.matmul(out, RBb[:, z, j], Uc[:, z, j], start=False, stop=True)
                            mm.then_inc(y_mm[z], 1)
                            for j in range(NC4):
                                out = ps[:, 4 + z, j * C:(j + 1) * C]
                                pe.matmul(out, Ktb[:, z, j], Vc[:, z, j], start=True, stop=False)
                                mm = pe.matmul(out, Btb[:, z, j], Uc[:, z, j], start=False, stop=True)
                            mm.then_inc(sn_mm[z], 1)

            @block.scalar
            def _(act):
                act.wait_ge(zero4, 5)
                start_counts(act, tr_ok, xt_ok, uc_ok)
                for t0, n, s0 in spans:
                    if t0:
                        act.wait_ge(so_mm, 1)
                        act.activation(stage_out, ps[:, 4:6, 0:NC4 * C].rearrange("p z (j n) -> p z j n", j=NC4), ACT.Copy).then_inc(so_ok, 1)
                    with act.Fori(0, n) as i:
                        s = i + s0
                        for z in range(2):
                            act.wait_ge(gT[z], s + 2)
                            for p in range(2):
                                act.activation(diag(Ktb[:, z], p), rows(quarter(GT), p), ACT.Copy)
                                act.activation(diag(Btb[:, z], p), rows(quarter(GT, 256), p), ACT.Copy, scale=-1.0)
                            act.activation(Vc[:, z], quarter(GV), ACT.Copy).then_inc(tr_ok[z], 1)
                        for l in range(LEVELS):
                            for z in range(2):
                                act.wait_ge(xt_mm[z], s * LEVELS + l + 2)
                                if l < LEVELS - 1:
                                    act.activation(XTc[:, z], quarter(4 + z), ACT.Copy)
                                act.activation(diag(XTb[:, z], 0), rows(quarter(4 + z), 0), ACT.Copy)
                                act.activation(diag(XTb[:, z], 1), rows(quarter(4 + z), 1), ACT.Copy).then_inc(xt_ok[z], 1)
                        for z in range(2):
                            act.wait_ge(u_mm[z], s + 2)
                            act.activation(Uc[:, z], quarter(4 + z), ACT.Copy).then_inc(uc_ok[z], 1)

            @block.vector
            def _(dve):
                dve.wait_ge(zero4, 5)
                start_counts(dve, lt_ok, rb_ok, rk_ok, z_ok, xc_ok, rh_ok, y_ok, s_add, s_ok)

                def eye(v, p=None):
                    m = istack if p is None else rows(istack, p)
                    return m.unsqueeze(1).to_broadcast([P if p is None else 64, NC4, C])

                def masked(dst, src, m):
                    for p in range(2):
                        ins = dve.tensor_tensor(diag(dst, p), rows(src, p), rows(m, p).unsqueeze(1).to_broadcast([64, NC4, C]), ALU.mult)
                    return ins

                for t0, n, s0 in spans:
                    if t0:
                        dve.wait_ge(si_mm, 1)
                        dve.tensor_copy(S, ps[:, 6:8, 0:NC4 * C].rearrange("p z (j n) -> p z j n", j=NC4)).then_inc(si_ok, 1)
                    with dve.Fori(0, n) as i:
                        s = i + s0
                        chunk = chunks(dve, i, t0, n, 1)
                        for z in range(2):
                            g1 = ps[:, GB, :].rearrange("p (j a t) -> p j a t", a=2, t=C)
                            g2 = ps[:, GK, :].rearrange("p (j a t) -> p j a t", a=2, t=C)
                            dve.wait_ge(gB[z], s + 2)
                            dve.wait_ge(lm_ok[z], s * LEVELS + 1)
                            for p in range(2):
                                ins = dve.tensor_copy(diag(LTb[:, z], p), rows(g1[:, :, 0], p))
                            ins.then_inc(lt_ok[z], 1)
                            masked(RBb[:, z], g1[:, :, 1], mnegincl[:, z]).then_inc(rb_ok[z], 1)
                            dve.wait_ge(gK[z], s + 2)
                            masked(MTb[:, z], g2[:, :, 0], mstrict[:, z])
                            masked(RKb[:, z], g2[:, :, 1], mincl[:, z]).then_inc(rk_ok[z], 1)
                        for l in range(LEVELS):
                            for z in range(2):
                                dve.wait_ge(w_mm[z], s * LEVELS + l + 2)
                                if l < LEVELS - 1:
                                    dve.tensor_tensor((Xc if l == 0 else Zc)[:, z], quarter(4 + z), eye(0), ALU.add)
                                for p in range(2):
                                    ins = dve.tensor_tensor(diag(Zb[:, z], p), rows(quarter(4 + z), p), eye(0, p), ALU.add)
                                ins.then_inc(z_ok[z], 1)
                            if 1 <= l < LEVELS - 1:
                                for z in range(2):
                                    dve.wait_ge(xq_mm[z], s * 4 + l + 1)
                                    dve.tensor_copy(Xc[:, z], quarter(6 + z)).then_inc(xc_ok[z], 1)
                        for z in range(2):
                            dve.wait_ge(rhs_mm[z], s + 2)
                            dve.tensor_copy(RHc[:, z], quarter(6 + z)).then_inc(rh_ok[z], 1)
                        for z in range(2):
                            dve.wait_ge(y_mm[z], s + 2)
                            dve.wait_ge(y_ok[z], s + 1)
                            dve.wait_ge(y_ok[1 - z], (s if z == 0 else s + 1) + 1)
                            ya = yacc[:, bass.ds(chunk[z], 1)].squeeze(1)
                            dve.tensor_tensor(ya, ya, quarter(6 + z), ALU.add).then_inc(y_ok[z], 1)
                            dve.wait_ge(sn_mm[z], s + 2)
                            dve.tensor_tensor(S[:, z], S[:, z], quarter(4 + z), ALU.add).then_inc(s_add[z], 1)
                            dve.wait_ge(s_add[z], s + 2)
                            pc_ = pc_all[:, z, :, bass.ds(chunk[z], 1)].to_broadcast([P, NC4, C])
                            dve.tensor_tensor(S[:, z], S[:, z], pc_, ALU.mult).then_inc(s_ok[z], 1)

        catT = view(CB, 2 * NC4, T)
        h2T = catT
        bmodA, g2row = view(CB + 8 * T, 4, 512), view(CB + 8 * T + 2048, D)
        assert 8 * T + 2048 + D <= 13 * T
        bmodB = lorabd
        modrow2 = view(CB + NET * T + NCH * NC4 * C, 2, 512)
        at = R
        bonus2 = view(at, NC4, T)
        yn = view(at + NC4 * T, NCH, NC4, C)
        h2 = view(at, NTT, D); at += NTT * D
        ring2 = view(at, 3, KT, 512); at += 3 * KT * 512
        gate1, shift2, gain2 = (view(at + i * 2 * D, 2, D) for i in range(3)); at += 6 * D
        tmp5 = view(at, 2, D)
        at5 = at + 2 * D
        XS = 53000 - NTT * D
        xs2 = view(XS, NTT, D)
        gate2 = view(XS - 2 * D, 2, D)
        assert at + NTT * 0 <= XS - 2 * D, (at, XS)
        tmp5 = view(CB + NET * T, 2, D)
        free0 = _CONST["levels"][0] + 0
        lv = [free0]

        def small_view(*shape):
            v = view(lv[0], *shape)
            lv[0] += int(np.prod(shape))
            assert lv[0] <= free0 + 2 * LEVELS * P
            return v

        gmean, gvar = small_view(NCH * NC4), small_view(NCH * NC4)
        logits = small_view(NTT, NG + NE)
        mxc, m2c, gsum, m1f, m2f, e2 = (small_view(NTT) for _ in range(6))
        eqc, ghot, expc, lsel, eq1, hot1, l2, hot2 = (small_view(NTT, 4) for _ in range(8))
        prod = small_view(NTT, NE)
        E1, E2, Msum, posn = (small_view(NTT, NE) for _ in range(4))
        cnt, ntile, incl, base, one16 = (small_view(NE) for _ in range(5))
        cmp = small_view(NT, NE)
        eid_f = small_view(NT)

        chunk2 = [(w_mod[0][:, 512 * j:512 * (j + 1)]) for j in range(4, 12)] + [w_out[0][:, 0:512], w_out[0][:, 512:]]
        (ld_ring20, ld_ring21, ld_ring22, ld_in5, ld_rows5, used2, mr_mm, mr_ok, mb_mm, mb_ok, gm_ok, gsq_ok, gv_ok,
         gs_ok, yn_ok, yT_mm, g_mm, cat_ok, mix_mm, x2_ok, ss_ok, v2_ok, sd2_ok, h2_ok, h2T_mm, h2T_ok, lg_mm, lgs_ok,
         ec_ok, ex_ok, d2_ok, e2_ok, m_ok, rank_mm, slot_ok, scattered, dve5, act5) = (sem(n) for n in (
             "ld_ring2_0", "ld_ring2_1", "ld_ring2_2", "ld_in5", "ld_rows5", "used2", "mr_mm", "mr_ok", "mb_mm",
             "mb_ok", "gm_ok", "gsq_ok", "gv_ok", "gs_ok", "yn_ok", "yT_mm", "g_mm", "cat_ok", "mix_mm", "x2_ok",
             "ss_ok", "v2_ok", "sd2_ok", "h2_ok", "h2T_mm", "h2T_ok", "lg_mm", "lgs_ok", "ec_ok", "ex_ok", "d2_ok",
             "e2_ok", "m_ok", "rank_mm", "slot_ok", "scattered", "dve5", "act5"))
        ld_ring2 = [ld_ring20, ld_ring21, ld_ring22]
        mods2 = (gate1, shift2, gain2, gate2)

        with nc.Block() as block:
            @block.sync
            def _(sp):
                for n, src in enumerate(chunk2):
                    if n >= 3:
                        sp.wait_ge(used2, n - 2)
                    sp.dma_start(ring2[:, n % 3], src.rearrange("(k p) n -> p k n", p=P)).then_inc(ld_ring2[n % 3], 16)
                sp.wait_ge(slot_ok, 1)

            @block.gpsimd
            def _(pool):
                pool.wait_ge(slot_ok, 1)
                for tt in range(NTT):
                    for r in range(2):
                        pool.indirect_dma_start(
                            out=xg_d, out_offset=bass.IndirectOffsetOnAxis(ap=slot_i[:, r * NTT + tt:r * NTT + tt + 1], axis=0),
                            in_=h2[:, tt, :], in_offset=None).then_inc(scattered, 16)
                pool.wait_ge(scattered, 32 * NTT)

            @block.scalar
            def _(act):
                for j in range(4):
                    for rows_, first in ((bmodA, 4), (bmodB.rearrange("p a b -> p (a b)").rearrange("p (a b) -> p a b", a=4), 8)):
                        lo = 512 * (first + j)
                        act.dma_start(rows_[0:2, j, :], b_mod[0, lo:lo + 512].partition_broadcast(2)).then_inc(ld_rows5, 16)
                act.dma_start(g2row[0:2, :], norm2_g[0].partition_broadcast(2)).then_inc(ld_rows5, 16)
                act.dma_start(bonus2.rearrange("p a t -> p (a t)"), bonus_d).then_inc(ld_in5, 16)
                act.dma_start(catT[:, 0:NC4].rearrange("p a t -> p (a t)"), attn_d).then_inc(ld_in5, 16)
                for tt in range(NTT):
                    src_x = x_prompt[0] if tt == 0 else x_sample[0, (tt - 1) * P:tt * P, :]
                    act.dma_start(xs2[:, tt, :], src_x).then_inc(ld_in5, 16)
                act.wait_ge(gm_ok, 1)
                act.activation(yn, yacc, ACT.Square).then_inc(gsq_ok, 1)
                act.wait_ge(gv_ok, 1)
                act.activation(gvar, gvar, ACT.Sqrt).then_inc(gs_ok, 1)
                n = 0
                for j in range(8):
                    for cc in range(2):
                        act.wait_ge(mb_mm, n + 1)
                        act.activation(mods2[j // 2][:, cc, 512 * (j % 2):512 * (j % 2 + 1)], ps[:, 6 + n % 2, :], ACT.Copy).then_inc(mb_ok, 1)
                        n += 1
                ch = Chain(act, act5)
                for tt in range(NTT):
                    act.wait_ge(x2_ok, tt + 1)
                    ins = act.activation(ps[:, 4:6, :], xs2[:, tt, :].rearrange("p (b n) -> p b n", b=2), ACT.Square, accum_out=ssq[:, tt:tt + 1])
                    ins.then_inc(ss_ok, 1)
                    act.wait_ge(ss_ok, tt + 1)
                act.wait_ge(v2_ok, 1)
                act.activation(rstd, ssq, ACT.Sqrt).then_inc(sd2_ok, 1)
                for tt in range(NTT):
                    act.wait_ge(h2T_mm, tt + 1)
                    b = 2 * (tt % 2)
                    act.activation(h2T[:, :, tt * P:(tt + 1) * P],
                                   ps[:, b:b + 2, :].rearrange("p b (k t) -> p (b k) t", t=P), ACT.Copy).then_inc(h2T_ok, 1)
                act.wait_ge(ec_ok, 1)
                act.activation(expc, expc, ACT.Exp).then_inc(ex_ok, 1)
                act.wait_ge(d2_ok, 1)
                act.activation(e2, e2, ACT.Exp).then_inc(e2_ok, 1)

            @block.tensor
            def _(pe):
                def mod_chunk(j):
                    pe.wait_ge(ld_ring2[j % 3], 16 * (j // 3 + 1))
                    if j >= 2:
                        pe.wait_ge(mr_ok, j - 1)
                    for k in range(KT):
                        mm = pe.matmul(ps[0:2, 4 + j % 2, :], cond2[:, k, :], ring2[:, j % 3, k, :], start=(k == 0), stop=(k == KT - 1))
                    mm.then_inc(mr_mm, 1)
                    pe.wait_ge(mr_mm, j + 1)
                    pe.nop().then_inc(used2, 1)

                def mod_rows(j):
                    pe.wait_ge(mr_ok, j + 1)
                    for cc in range(2):
                        n = 2 * j + cc
                        if n >= 2:
                            pe.wait_ge(mb_ok, n - 1)
                        pe.matmul(ps[:, 6 + n % 2, :], sel[0:2, cc, :], modrow2[0:2, j % 2, :], start=True, stop=True).then_inc(mb_mm, 1)

                def turn(c4):
                    if c4 >= 1:
                        pe.wait_ge(cat_ok, c4)
                    for ch_i in range(NCH):
                        for p in range(2):
                            mm = pe.matmul(ps[64 * p:64 * p + 64, ch_i // 5, (ch_i % 5) * C:(ch_i % 5 + 1) * C],
                                           rows(yn[:, ch_i, c4], p), rows(istack, p), start=True, stop=True)
                    mm.then_inc(yT_mm, 1)
                    for hf in range(2):
                        mm = pe.matmul(ps[:, 2 + hf, 0:T // 2], glora[0:GATE_LORA, c4 * P:(c4 + 1) * P],
                                       gate_in[0:GATE_LORA, hf * T // 2:(hf + 1) * T // 2], start=True, stop=True)
                    mm.then_inc(g_mm, 1)

                mod_chunk(0)
                for j in range(1, 8):
                    mod_chunk(j)
                    mod_rows(j - 1)
                    if j == 2:
                        pe.wait_ge(yn_ok, 1)
                    if 2 <= j < 6:
                        turn(j - 2)
                mod_rows(7)
                pe.wait_ge(cat_ok, NC4)
                pe.wait_ge(ld_in5, 16 * 7)
                pe.wait_ge(ld_ring2[8 % 3], 16 * 3)
                pe.wait_ge(ld_ring2[9 % 3], 16 * 4)
                for tt in range(NTT):
                    b = 2 * (tt % 2)
                    if tt >= 2:
                        pe.wait_ge(x2_ok, tt - 1)
                    for half in range(2):
                        for k in range(KT):
                            mm = pe.matmul(ps[:, b + half, :], catT[:, k, tt * P:(tt + 1) * P], ring2[:, (8 + half) % 3, k, :],
                                           start=(k == 0), stop=(k == KT - 1))
                    mm.then_inc(mix_mm, 1)
                for tt in range(NTT):
                    pe.wait_ge(h2_ok, tt + 1)
                    b = 2 * (tt % 2)
                    if tt >= 2:
                        pe.wait_ge(h2T_ok, tt - 1)
                    for k in range(KT):
                        mm = pe.transpose(ps[:, b + k // 4, (k % 4) * P:(k % 4 + 1) * P], h2[:, tt, k * P:(k + 1) * P], ident)
                    mm.then_inc(h2T_mm, 1)
                pe.wait_ge(h2T_ok, NTT)
                for tt in range(NTT):
                    for k in range(KT):
                        mm = pe.matmul(ps[:, 6, tt * 32:tt * 32 + NG + NE], h2T[:, k, tt * P:(tt + 1) * P], router[:, k, :],
                                       start=(k == 0), stop=(k == KT - 1))
                mm.then_inc(lg_mm, 1)
                pe.wait_ge(m_ok, 1)
                for tt in range(NTT + 1):
                    out = ps[:, 7, tt * NE:(tt + 1) * NE]
                    for t2 in range(min(tt, NTT)):
                        mm = pe.matmul(out, ones, Msum[:, t2, :], start=(t2 == 0), stop=(tt == NTT and t2 == NTT - 1))
                    if tt < NTT:
                        mm = pe.matmul(out, stricttri, Msum[:, tt, :], start=(tt == 0), stop=True)
                mm.then_inc(rank_mm, 1)

            @block.vector
            def _(dve):
                ch = Chain(dve, dve5)

                def bc(v, n):
                    return v.unsqueeze(2).to_broadcast([P, v.shape[1], n])

                ya = yacc.rearrange("p a b c -> p (a b) c")
                yb = yn.rearrange("p a b c -> p (a b) c")
                ch(dve.tensor_reduce(gmean, ya, AX.X, ALU.add))
                ch(dve.tensor_scalar(gmean, gmean, 1.0 / C, None, ALU.mult))
                dve.tensor_tensor(ya, ya, bc(gmean, C), ALU.subtract).then_inc(gm_ok, 1)
                dve.wait_ge(gsq_ok, 1)
                ch(dve.tensor_reduce(gvar, yb, AX.X, ALU.add))
                dve.tensor_scalar(gvar, gvar, 1.0 / C, GN_EPS, ALU.mult, ALU.add).then_inc(gv_ok, 1)
                dve.wait_ge(gs_ok, 1)
                ch(dve.reciprocal(gvar, gvar))
                dve.tensor_tensor(yb, ya, bc(gvar, C), ALU.mult).then_inc(yn_ok, 1)
                dve.wait_ge(ld_rows5, 16 * 9)
                dve.wait_ge(ld_in5, 16 * 7)
                bB = bmodB.rearrange("p a b -> p (a b)").rearrange("p (a b) -> p a b", a=4)

                def mod_row(j):
                    dve.wait_ge(mr_mm, j + 1)
                    if j >= 2:
                        dve.wait_ge(mb_mm, 2 * (j - 1))
                    row = modrow2[0:2, j % 2, :]
                    bm = (bmodA if j < 4 else bB)[0:2, j % 4, :]
                    if j // 2 != 2:
                        dve.tensor_tensor(row, ps[0:2, 4 + j % 2, :], bm, ALU.add).then_inc(mr_ok, 1)
                    else:
                        ch(dve.tensor_tensor(row, ps[0:2, 4 + j % 2, :], bm, ALU.add))
                        dve.scalar_tensor_tensor(row, row, 1.0, g2row[0:2, 512 * (j - 4):512 * (j - 3)], ALU.add, ALU.mult).then_inc(mr_ok, 1)

                def cat(c4):
                    t5 = tmp5.rearrange("p a b -> p (a b)")[:, 0:T]
                    dve.wait_ge(yT_mm, c4 + 1)
                    ch(dve.tensor_scalar(halves(t5), two_banks(0), lngv[:, c4:c4 + 1], lnbv[:, c4:c4 + 1], ALU.mult, ALU.add))
                    ch(dve.tensor_tensor(t5, t5, bonus2[:, c4, :], ALU.add))
                    dve.wait_ge(g_mm, c4 + 1)
                    dve.tensor_tensor(halves(catT[:, NC4 + c4, :]), halves(t5), two_banks(2), ALU.mult).then_inc(cat_ok, 1)

                for j in range(8):
                    mod_row(j)
                    if 2 <= j < 6:
                        cat(j - 2)
                dve.wait_ge(mb_ok, 16)
                for tt in range(NTT):
                    cc = 0 if tt == 0 else 1
                    dve.wait_ge(mix_mm, tt + 1)
                    b = 2 * (tt % 2)
                    ch(dve.tensor_tensor(tmp5[:, tt % 2, :].rearrange("p (b n) -> p b n", b=2), ps[:, b:b + 2, :],
                                         gate1[:, cc, :].rearrange("p (b n) -> p b n", b=2), ALU.mult))
                    dve.tensor_tensor(xs2[:, tt, :], xs2[:, tt, :], tmp5[:, tt % 2, :], ALU.add).then_inc(x2_ok, 1)
                dve.wait_ge(ss_ok, NTT)
                dve.tensor_scalar(ssq, ssq, 1.0 / D, EPS, ALU.mult, ALU.add).then_inc(v2_ok, 1)
                dve.wait_ge(sd2_ok, 1)
                ch(dve.reciprocal(rstd, rstd))
                for tt in range(NTT):
                    cc = 0 if tt == 0 else 1
                    ch(dve.scalar_tensor_tensor(h2[:, tt, :], xs2[:, tt, :], rstd[:, tt:tt + 1], gain2[:, cc, :], ALU.mult, ALU.mult))
                    dve.tensor_tensor(h2[:, tt, :], h2[:, tt, :], shift2[:, cc, :], ALU.add).then_inc(h2_ok, 1)
                prio_b = cst("prio").unsqueeze(1).to_broadcast([P, NTT, 4])

                def first_max(hot, eq, vals, mx, m2):
                    ch(dve.tensor_reduce(mx, vals, AX.X, ALU.max))
                    ch(dve.tensor_tensor(eq, vals, bc(mx, 4), ALU.is_equal))
                    ch(dve.tensor_tensor(eq, eq, prio_b, ALU.mult))
                    ch(dve.tensor_reduce(m2, eq, AX.X, ALU.max))
                    ch(dve.tensor_tensor(hot, eq, bc(m2, 4), ALU.is_equal))

                ch(dve.memset(one16, 1.0))
                dve.wait_ge(lg_mm, 1)
                ch(dve.tensor_tensor(logits, ps[:, 6, 0:NTT * 32].rearrange("p (t n) -> p t n", n=32)[:, :, 0:NG + NE],
                                     rbias.unsqueeze(1).to_broadcast([P, NTT, NG + NE]), ALU.add))
                lc = logits[:, :, 0:NG]
                first_max(ghot, eqc, lc, mxc, m2c)
                dve.tensor_tensor(expc, lc, bc(mxc, 4), ALU.subtract).then_inc(ec_ok, 1)
                dve.wait_ge(ex_ok, 1)
                ch(dve.tensor_reduce(gsum, expc, AX.X, ALU.add))
                p4 = prod.rearrange("p t (g e) -> p t g e", g=NG)
                for g in range(NG):
                    ins = dve.tensor_tensor(p4[:, :, g, :], logits[:, :, NG + 4 * g:NG + 4 * g + 4],
                                            ghot[:, :, g:g + 1].to_broadcast([P, NTT, 4]), ALU.mult)
                ch(ins)
                ch(dve.tensor_reduce(lsel, prod.rearrange("p t (g e) -> p t e g", g=NG), AX.X, ALU.add))
                first_max(hot1, eq1, lsel, m1f, m2c)
                ch(dve.scalar_tensor_tensor(l2, hot1, -BIG, lsel, ALU.mult, ALU.add))
                first_max(hot2, eq1, l2, m2f, m2c)
                dve.tensor_tensor(e2, m2f, m1f, ALU.subtract).then_inc(d2_ok, 1)
                dve.wait_ge(e2_ok, 1)
                ch(dve.tensor_scalar(m1f, e2, 1.0, None, ALU.add))
                ch(dve.tensor_tensor(m1f, m1f, gsum, ALU.mult))
                ch(dve.reciprocal(wsel[:, 0, :], m1f))
                ch(dve.tensor_tensor(wsel[:, 1, :], wsel[:, 0, :], e2, ALU.mult))
                for E_, hot in ((E1, hot1), (E2, hot2)):
                    for g in range(NG):
                        ins = dve.tensor_tensor(E_[:, :, 4 * g:4 * g + 4], hot, ghot[:, :, g:g + 1].to_broadcast([P, NTT, 4]), ALU.mult)
                ch(ins)
                dve.tensor_tensor(Msum, E1, E2, ALU.add).then_inc(m_ok, 1)
                dve.wait_ge(rank_mm, 1)
                ch(dve.tensor_copy(cnt, ps[:, 7, NTT * NE:(NTT + 1) * NE]))
                ch(dve.tensor_scalar(ntile, cnt, 0.0, None, ALU.is_gt))
                for j in range(1, NTT):
                    ch(dve.scalar_tensor_tensor(ntile, cnt, float(P * j), ntile, ALU.is_gt, ALU.add))
                ch(dve.tensor_tensor_scan(incl, one16, ntile, 0.0, ALU.mult, ALU.add))
                ch(dve.tensor_tensor(base, incl, ntile, ALU.subtract))
                ch(dve.tensor_scalar(base, base, float(P), None, ALU.mult))
                ch(dve.tensor_tensor(posn, ps[:, 7, 0:NTT * NE].rearrange("p (t e) -> p t e", e=NE),
                                     base.unsqueeze(1).to_broadcast([P, NTT, NE]), ALU.add))
                for r, E_ in enumerate((E1, E2)):
                    ch(dve.tensor_tensor(prod, E_, posn, ALU.mult))
                    ch(dve.tensor_reduce(slot_f[:, r, :], prod, AX.X, ALU.add))
                ch(dve.tensor_copy(slot_i[:, :], slot_f.rearrange("p r t -> p (r t)")))
                ch(dve.tensor_tensor(cmp, incl.unsqueeze(1).to_broadcast([P, NT, NE]), cst("tile_iota").unsqueeze(2).to_broadcast([P, NT, NE]), ALU.is_le))
                ch(dve.tensor_reduce(eid_f, cmp, AX.X, ALU.add))
                ch(dve.tensor_scalar(eid_f, eid_f, float(NE - 1), None, ALU.min))
                dve.tensor_copy(eid_i[:, :], eid_f).then_inc(slot_ok, 1)

        at = CB
        wg, wu = view(at, 2, KT, FE), view(at + 2 * KT * FE, 2, KT, FE); at += 4 * KT * FE
        wd = view(at, 2, 4, D); at += 8 * D
        xg = view(at, 2, D); at += 2 * D
        xgT = view(at, KT, P); at += KT * P
        sg, hid = view(at, FE), view(at + FE, FE); at += 2 * FE
        hidT = view(at, 4, P); at += 4 * P
        yo = view(at, 2, D); at += 2 * D
        assert at <= XS - 2 * D
        ld_xg, ld_gu, ld_wd, y_st = ([sem(f"{n}_{u}") for u in range(2)] for n in ("ld_xg", "ld_gu", "ld_wd", "y_stored"))
        (xgT_mm, xgT_ok, g6_mm, u6_mm, sg_ok, hsg_ok, hid_ok, hT6_mm, hT6_ok, y6_mm, yo_a, yo_v) = (sem(n) for n in (
            "xgT_mm", "xgT_ok", "gate_mm", "up_mm", "sig6_ok", "gsig_ok", "hid_ok", "hidT_mm", "hidT_ok", "down_mm",
            "yo_act", "yo_dve"))
        GA, UP, XT0, HT, Y0 = 0, 1, 2, 4, 5

        with nc.Block() as block:
            @block.sync
            def _(sp):
                def load(i, u):
                    e = sp.value_load(eid_i[0:1, bass.ds(i, 1)] if not isinstance(i, int) else eid_i[0:1, i:i + 1], min_val=0, max_val=NE - 1)
                    sp.dma_start(wg[:, u], exp_gate[0][bass.ds(e, 1)].squeeze(0).rearrange("(k p) n -> p k n", p=P)).then_inc(ld_gu[u], 16)
                    sp.dma_start(wu[:, u], exp_up[0][bass.ds(e, 1)].squeeze(0).rearrange("(k p) n -> p k n", p=P)).then_inc(ld_gu[u], 16)
                    return e

                def load_down(e, u):
                    sp.dma_start(wd[:, u], exp_down[0][bass.ds(e, 1)].squeeze(0).rearrange("(k p) n -> p k n", p=P)).then_inc(ld_wd[u], 16)

                def load_x(i, u):
                    sp.dma_start(xg[:, u], xg_d[bass.ds(i * P, P), :]).then_inc(ld_xg[u], 16)

                for i in range(2):
                    load_x(i, i)
                    load_down(load(i, i), i)

                def step(i, u):
                    sp.wait_ge(xgT_mm, i - 1)
                    load_x(i, u)
                    sp.wait_ge(u6_mm, i - 1)
                    e = load(i, u)
                    sp.wait_ge(y6_mm, i - 1)
                    load_down(e, u)

                with sp.Fori(0, (NT - 3) // 2) as j:
                    for u in range(2):
                        step(j * 2 + (2 + u), u)
                step(NT - 1, (NT - 1) % 2)
                sp.wait_ge(xgT_mm, NT - 1)
                load_x(NT, NT % 2)
                sp.wait_ge(ld_xg[NT % 2], 16 * (NT // 2 + 1))

            @block.tensor
            def _(pe):
                def x_turn(i, u, n):
                    pe.wait_ge(ld_xg[u], n)
                    for k in range(KT):
                        mm = pe.transpose(ps[:, XT0 + k // 4, (k % 4) * P:(k % 4 + 1) * P], xg[:, u, k * P:(k + 1) * P], ident)
                    mm.then_inc(xgT_mm, 1)

                def gate_up(i, u, n):
                    pe.wait_ge(ld_gu[u], n)
                    pe.wait_ge(xgT_ok, i + 1)
                    for w, b, s_ in ((wg, GA, g6_mm), (wu, UP, u6_mm)):
                        for k in range(KT):
                            mm = pe.matmul(ps[:, b, :], xgT[:, k, :], w[:, u, k, :], start=(k == 0), stop=(k == KT - 1))
                        mm.then_inc(s_, 1)

                def h_turn(i):
                    pe.wait_ge(hid_ok, i + 1)
                    for k in range(4):
                        mm = pe.transpose(ps[:, HT, k * P:(k + 1) * P], hid[:, k * P:(k + 1) * P], ident)
                    mm.then_inc(hT6_mm, 1)

                def down(i, u, n):
                    pe.wait_ge(ld_wd[u], n)
                    pe.wait_ge(hT6_ok, i + 1)
                    for half in range(2):
                        for k in range(4):
                            mm = pe.matmul(ps[:, Y0 + half, :], hidT[:, k, :], wd[:, u, k, half * 512:(half + 1) * 512],
                                           start=(k == 0), stop=(k == 3))
                    mm.then_inc(y6_mm, 1)

                x_turn(0, 0, 16)
                gate_up(0, 0, 32)
                x_turn(1, 1, 16)
                with pe.Fori(0, (NT - 1) // 2) as j:
                    for u in (1, 0):
                        i = j * 2 + (2 - u)
                        h_turn(i - 1)
                        gate_up(i, u, (j * 32) + (32 if u else 64))
                        x_turn(i + 1, 1 - u, (j * 16) + 32)
                        pe.wait_ge(yo_a, i)
                        pe.wait_ge(yo_v, i)
                        down(i - 1, 1 - u, (j * 16) + 16)
                h_turn(NT - 1)
                pe.wait_ge(yo_a, NT)
                pe.wait_ge(yo_v, NT)
                down(NT - 1, (NT - 1) % 2, 16 * ((NT - 1) // 2 + 1))

            @block.scalar
            def _(act):
                def sigmoid(i):
                    act.wait_ge(g6_mm, i + 1)
                    act.activation(sg, ps[:, GA, :], ACT.Sigmoid).then_inc(sg_ok, 1)

                def x_out(i):
                    act.wait_ge(xgT_mm, i + 1)
                    act.activation(xgT, ps[:, XT0:XT0 + 2, :].rearrange("p b (k t) -> p (b k) t", t=P), ACT.Copy).then_inc(xgT_ok, 1)

                def h_out(i):
                    act.wait_ge(hT6_mm, i + 1)
                    act.activation(hidT, ps[:, HT, :].rearrange("p (k t) -> p k t", t=P), ACT.Copy).then_inc(hT6_ok, 1)

                def y_out(i, u, n):
                    act.wait_ge(y6_mm, i + 1)
                    act.wait_ge(y_st[u], n)
                    act.activation(yo[:, u, 0:512], ps[:, Y0, :], ACT.Copy).then_inc(yo_a, 1)
                    act.wait_ge(yo_a, i + 2)
                    act.wait_ge(yo_v, i + 2)
                    act.dma_start(yg_d[bass.ds(i * P, P), :], yo[:, u]).then_inc(y_st[u], 16)

                act.nop().then_inc(yo_a, 1)
                act.nop().then_inc(y_st[0], 16)
                act.nop().then_inc(y_st[1], 16)
                x_out(0)
                sigmoid(0)
                x_out(1)
                with act.Fori(0, (NT - 1) // 2) as j:
                    for u in (1, 0):
                        i = j * 2 + (2 - u)
                        h_out(i - 1)
                        sigmoid(i)
                        x_out(i + 1)
                        y_out(i - 1, 1 - u, j * 16 + 16)
                h_out(NT - 1)
                y_out(NT - 1, 0, 16 * ((NT - 1) // 2) + 16)
                act.wait_ge(y_st[0], 16 * ((NT + 1) // 2) + 16)
                act.wait_ge(y_st[1], 16 * (NT // 2) + 16)

            @block.vector
            def _(dve):
                def hidden(i):
                    dve.wait_ge(sg_ok, i + 1)
                    dve.tensor_tensor(sg, sg, ps[:, GA, :], ALU.mult).then_inc(hsg_ok, 1)
                    dve.wait_ge(hsg_ok, i + 1)
                    dve.wait_ge(u6_mm, i + 1)
                    dve.tensor_tensor(hid, sg, ps[:, UP, :], ALU.mult).then_inc(hid_ok, 1)

                def y_out(i, u, n):
                    dve.wait_ge(y6_mm, i + 1)
                    dve.wait_ge(y_st[u], n)
                    dve.tensor_copy(yo[:, u, 512:], ps[:, Y0 + 1, :]).then_inc(yo_v, 1)

                dve.nop().then_inc(yo_v, 1)
                hidden(0)
                with dve.Fori(0, (NT - 1) // 2) as j:
                    for u in (1, 0):
                        i = j * 2 + (2 - u)
                        hidden(i)
                        y_out(i - 1, 1 - u, j * 16 + 16)
                y_out(NT - 1, 0, 16 * ((NT - 1) // 2) + 16)

        yA, yB = view(CB, NTT, D), view(CB + NTT * D, NTT, D)
        got, y7, st7, dve7 = [sem(f"gathered_{tt}") for tt in range(NTT)], sem("y7"), sem("st7"), sem("dve7")

        with nc.Block() as block:
            @block.gpsimd
            def _(pool):
                for tt in range(NTT):
                    for r, dst in enumerate((yA, yB)):
                        pool.indirect_dma_start(
                            out=dst[:, tt, :], out_offset=None, in_=yg_d,
                            in_offset=bass.IndirectOffsetOnAxis(ap=slot_i[:, r * NTT + tt:r * NTT + tt + 1], axis=0)).then_inc(got[tt], 16)

            @block.vector
            def _(dve):
                ch = Chain(dve, dve7)
                for tt in range(NTT):
                    cc = 0 if tt == 0 else 1
                    dve.wait_ge(got[tt], 32)
                    ch(dve.tensor_scalar(yA[:, tt, :], yA[:, tt, :], wsel[:, 0, tt:tt + 1], None, ALU.mult))
                    ch(dve.scalar_tensor_tensor(yA[:, tt, :], yB[:, tt, :], wsel[:, 1, tt:tt + 1], yA[:, tt, :], ALU.mult, ALU.add))
                    ch(dve.tensor_tensor(yA[:, tt, :], yA[:, tt, :], gate2[:, cc, :], ALU.mult))
                    dve.tensor_tensor(yA[:, tt, :], yA[:, tt, :], xs2[:, tt, :], ALU.add).then_inc(y7, 1)

            @block.sync
            def _(sp):
                for tt in range(NTT):
                    sp.wait_ge(y7, tt + 1)
                    dst = y_prompt[0] if tt == 0 else y_sample[0, (tt - 1) * P:tt * P, :]
                    sp.dma_start(dst, yA[:, tt, :]).then_inc(st7, 16)
                sp.wait_ge(st7, 16 * NTT)


_INS = ['x_prompt', 'x_sample', 'cache_k', 'cache_v', 'state_rwkv', 'c', 'c_ctx', 'w_mod', 'b_mod', 'norm1_g',
        'norm2_g', 'w_in', 'mu_shift', 'q_norm_g', 'k_norm_g', 'w0', 'w_lora_up', 'a0', 'a_lora_up', 'g_lora_up',
        'k_k', 'k_a', 'r_k', 'ln_x_g', 'ln_x_b', 'w_out', 'router_c', 'router_c_b', 'router_f', 'router_f_b',
        'exp_gate', 'exp_up', 'exp_down']
_OUTS = [((1, T_CTX, D), 'float32'), ((1, T_LAT, D), 'float32'), ((1, 1, T_CTX, NKV, HD), 'float32'),
         ((1, 1, T_CTX, NKV, HD), 'float32'), ((1, 1, 2, 8, HD, HD), 'float32')]


def kernel(**inputs):
    import numpy as _np
    import concourse.bacc as _bacc
    from concourse import mybir as _mybir
    from concourse.bass_utils import run_bass_kernel_spmd as _run

    nc = _bacc.Bacc("TRN2", target_bir_lowering=False, num_devices=1)
    arrays, args = {}, []
    for name in _INS + ['consts']:
        a = const_table() if name == 'consts' else _np.ascontiguousarray(inputs[name])
        arrays[f"in_{name}_dram"] = a
        args.append(nc.dram_tensor(f"in_{name}_dram", a.shape, _mybir.dt.from_np(a.dtype), kind="ExternalInput").ap())
    for i, (shape, dtype) in enumerate(_OUTS):
        dt = _mybir.dt.from_np(_np.dtype(dtype))
        args.append(nc.dram_tensor(f"out_{i}_dram", shape, dt, kind="ExternalOutput").ap())
    build(nc, *args)
    r = _run(nc, [arrays], core_ids=[0])
    return tuple(r.results[0][f"out_{i}_dram"] for i in range(len(_OUTS)))
```

```python
from contextlib import ExitStack

import numpy as np
import concourse.bass as bass
from concourse import mybir

F32 = mybir.dt.float32
I32 = mybir.dt.int32
ACT = mybir.ActivationFunctionType
ALU = mybir.AluOpType
AX = mybir.AxisListType

P = 128
D = 1024
KT = D // P
T_CTX, T_LAT = 128, 512
T = T_CTX + T_LAT
NTT = T // P
HD = 64
NQ, NKV = 8, 2
D_ATTN = NQ * HD
D_KV = NKV * HD
D_QKV = D_ATTN + 2 * D_KV
PAST = 128
D_RWKV = 512
NC4 = D_RWKV // P
LORA_IN = 128
GATE_LORA = 96
NET = 14
C = 64
NCH = T // C
DS = 0.6065306597
LEVELS = 6
NG, EPG, NE = 4, 4, 16
FE = 512
NT = 25
MIN_TILES = T * 2 // P
EPS = 1e-6
GN_EPS = 64e-5
GRID_W = 64
BIG = 3.0e38

_CONST = {}


def _const_cols():
    at = 0
    for name, n in (("ident", P), ("istack", C), ("ones", P), ("blockones", P), ("stricttri", P),
                    ("levels", 2 * LEVELS * C), ("mstrict", 2 * C), ("mincl", 2 * C), ("mnegincl", 2 * C),
                    ("rope_c", 4 * HD), ("rope_s", 4 * HD), ("scanmask", T), ("sel", 2 * P),
                    ("prio", 4), ("tile_iota", NT)):
        _CONST[name] = (at, n)
        at += n
    return at


NCONST = _const_cols()


def const_table():
    out = np.zeros((P, NCONST), np.float32)

    def put(name, value):
        a, n = _CONST[name]
        out[:, a:a + n] = np.asarray(value, np.float32).reshape(P, n)

    q = np.arange(P)
    half, pos = q // C, q % C
    put("ident", np.eye(P))
    put("istack", pos[:, None] == np.arange(C)[None])
    put("ones", np.ones((P, P)))
    same = half[:, None] == half[None]
    put("blockones", same)
    put("stricttri", q[:, None] < q[None])
    s, t = pos[:, None], np.arange(C)[None]
    lev = np.zeros((P, 2, LEVELS, C))
    for j in range(LEVELS):
        m = 2 ** j
        near = (s // (2 * m) == t // (2 * m)) & (s // m != t // m)
        lev[:, 0, j] = -1.0 * (near & (t > s))
        lev[:, 1, j] = -1.0 * (near & (t < s))
    put("levels", lev)
    tt = np.arange(C)[None]
    put("mstrict", np.stack([tt > s, tt < s], 1))
    put("mincl", np.stack([tt >= s, tt <= s], 1))
    put("mnegincl", -np.stack([tt >= s, tt <= s], 1).astype(np.float32))
    hh = HD // 2
    inv = (10000.0 ** (-np.arange(0, hh, 2, dtype=np.float32) / hh)).astype(np.float32)
    tok = np.arange(T_LAT)
    rc = np.zeros((T_LAT, HD), np.float32)
    rs = np.zeros((T_LAT, HD), np.float32)
    for g, where in enumerate((tok // GRID_W, tok % GRID_W)):
        ang = where.astype(np.float32)[:, None] * inv[None]
        rc[:, g * hh:(g + 1) * hh] = np.concatenate([np.cos(ang), np.cos(ang)], 1)
        rs[:, g * hh:(g + 1) * hh] = np.concatenate([-np.sin(ang), np.sin(ang)], 1)
    put("rope_c", rc.reshape(4, P, HD).transpose(1, 0, 2))
    put("rope_s", rs.reshape(4, P, HD).transpose(1, 0, 2))
    put("scanmask", np.broadcast_to(np.arange(T) % C != 0, (P, T)))
    sel = np.zeros((P, 2, P))
    sel[0, 0] = 1
    sel[1, 1] = 1
    put("sel", sel)
    put("prio", np.broadcast_to(np.array([4, 3, 2, 1]), (P, 4)))
    put("tile_iota", np.broadcast_to(np.arange(NT), (P, NT)))
    return out


class Chain:

    def __init__(self, eng, sem):
        self.eng, self.sem, self.n = eng, sem, 0

    def __call__(self, ins):
        self.n += 1
        ins.then_inc(self.sem, 1)
        self.eng.wait_ge(self.sem, self.n)


def build(nc, x_prompt, x_sample, cache_k, cache_v, state_rwkv, c, c_ctx, w_mod, b_mod, norm1_g, norm2_g, w_in,
          mu_shift, q_norm_g, k_norm_g, w0, w_lora_up, a0, a_lora_up, g_lora_up, k_k, k_a, r_k, ln_x_g, ln_x_b,
          w_out, router_c, router_c_b, router_f, router_f_b, exp_gate, exp_up, exp_down, consts,
          y_prompt, y_sample, new_cache_k, new_cache_v, new_state):
    ctx = ExitStack()
    with ctx:
        phase_sems = []

        def sem(name):
            one = nc.alloc_semaphore(name)
            phase_sems.append(one)
            return one

        top = [0]
        arena = ctx.enter_context(nc.sbuf_tensor("arena", [P, 53000], F32))
        ps = ctx.enter_context(nc.psum_tensor("ps", [P, 8, 512], F32))

        def view(at, *shape):
            n = int(np.prod(shape))
            assert at + n <= 53000, (at, n)
            v = arena[:, at:at + n]
            if len(shape) == 1:
                return v
            names = "abcdef"[:len(shape)]
            return v.rearrange("p (%s) -> p %s" % (" ".join(names), " ".join(names)), **dict(zip(names, shape)))

        def take(*shape):
            v = view(top[0], *shape)
            top[0] += int(np.prod(shape))
            return v

        const = take(NCONST)

        def cst(name, *shape):
            a, n = _CONST[name]
            v = const[:, a:a + n]
            if len(shape) < 2:
                return v
            names = "abcdef"[:len(shape)]
            return v.rearrange("p (%s) -> p %s" % (" ".join(names), " ".join(names)), **dict(zip(names, shape)))

        ident, istack, ones, blockones = cst("ident"), cst("istack"), cst("ones"), cst("blockones")
        stricttri = cst("stricttri")
        levels = cst("levels", 2, LEVELS, C)
        mstrict, mincl, mnegincl = cst("mstrict", 2, C), cst("mincl", 2, C), cst("mnegincl", 2, C)
        rope_c, rope_s = cst("rope_c", 4, HD), cst("rope_s", 4, HD)
        scanmask, sel = cst("scanmask"), cst("sel", 2, P)
        mu = take(2, NET)
        mu_c0 = take(NET)
        w0v, a0v = take(2, NC4), take(2, NC4)
        kkv, kav, ka1v, rkv, lngv, lnbv = (take(NC4) for _ in range(6))
        gq, gk = take(HD), take(HD)
        lorabd = take(4, D_RWKV)
        glora = take(D_RWKV)
        router = take(KT, NG + NE)
        rbias = take(NG + NE)
        ssq, rstd = take(NTT), take(NTT)
        pc_all = take(2, NC4, NCH)
        wsel = take(2, NTT)
        slot_f = take(2, NTT)
        cond2 = take(KT, 2)
        slot_i = ctx.enter_context(nc.sbuf_tensor("slot_i", [P, 2 * NTT], I32))
        eid_i = ctx.enter_context(nc.sbuf_tensor("eid_i", [P, NT + 1], I32))
        CB = top[0]

        rws = view(CB, NET, T)
        qkv = view(CB + NET * T, NTT, D_QKV)
        R = CB + NET * T + NTT * D_QKV

        attn_d = nc.dram_tensor("attn_scratch", (P, NC4 * T), F32, kind="Internal").ap()
        bonus_d = nc.dram_tensor("bonus_scratch", (P, NC4 * T), F32, kind="Internal").ap()
        xg_d = nc.dram_tensor("gathered_tokens", ((NT + 1) * P, D), F32, kind="Internal").ap()
        yg_d = nc.dram_tensor("expert_outputs", (NT * P, D), F32, kind="Internal").ap()

        at = R
        xs = view(at, NTT, D); at += NTT * D
        shift1 = view(at, 2, D); gain1 = view(at + 2 * D, 2, D); at += 4 * D
        ring = view(at, 3, KT, 512); at += 3 * KT * 512
        hT = view(at, KT, T); at += KT * T
        htmp = view(at, 2, D); at += 2 * D
        raw = view(at, 2, T + 4); at += 2 * (T + 4)
        cond = view(at, 2, KT, 2); at += 4 * KT
        modrow = view(at, 2, 512); at += 1024
        junk = htmp
        kcache, vcache = view(at, P), view(at + P, P); at += 2 * P

        chunk_src = [(w_mod[0][:, 512 * j:512 * (j + 1)], 512) for j in range(4)]
        for lo, hi in ((0, 512), (512, 768), (768, 1280), (1280, 1792), (1792, 2304), (2304, 2528)):
            chunk_src.append((w_in[0][:, lo:hi], hi - lo))

        ld_const, ld_x, ld_small, ld_ring0, ld_ring1, ld_ring2 = (
            sem(n) for n in ("ld_const", "ld_x", "ld_small", "ld_ring0", "ld_ring1", "ld_ring2"))
        ld_ring = [ld_ring0, ld_ring1, ld_ring2]
        ring_used, lora_zero, cond_ready, cond_sig = sem("ring_used"), sem("lora_zero"), sem("cond_ready"), sem("cond_sig")
        mu_ready = sem("mu_ready")
        modrow_mm, modrow_ok, bc_mm, bc_ok = sem("modrow_mm"), sem("modrow_ok"), sem("bc_mm"), sem("bc_ok")
        ld_bg, ld_cond = sem("ld_bg"), sem("ld_cond")
        ssq_ok, var_ok, std_ok, h_ok, hT_mm, hT_ok = (sem(n) for n in ("ssq_ok", "var_ok", "std_ok", "h_ok", "hT_mm", "hT_ok"))
        qkv_mm, q_ok, kv_ok, rw_mm, raw_ok, shift_ok = (sem(n) for n in ("qkv_mm", "q_ok", "kv_ok", "rw_mm", "raw_ok", "shift_ok"))
        st_cv, raw_zero = sem("st_cv"), sem("raw_zero")
        dve1, act1, pool1 = sem("dve1"), sem("act1"), sem("pool1")
        bmod2 = view(CB + NET * T, 4, 512)
        g1row = view(CB + NET * T + 2048, D)
        assert at <= 53000, at

        def col(v):
            return v.rearrange("(t p) -> p t", p=P)

        small = [
            (mu[:, 0, 0:13], col(mu_shift[0, 0, 0:13 * P])), (mu[:, 1, 0:13], col(mu_shift[0, 1, 0:13 * P])),
            (mu[0:96, 0, 13:14], mu_shift[0, 0, 13 * P:].rearrange("(p a) -> p a", a=1)),
            (mu[0:96, 1, 13:14], mu_shift[0, 1, 13 * P:].rearrange("(p a) -> p a", a=1)),
            (kkv, col(k_k[0])), (kav, col(k_a[0])), (rkv, col(r_k[0].rearrange("h k -> (h k)"))),
            (lngv, col(ln_x_g[0])), (lnbv, col(ln_x_b[0])),
            (gq, q_norm_g[0].partition_broadcast(P)), (gk, k_norm_g[0].partition_broadcast(P)),
            (glora[0:GATE_LORA, :], g_lora_up[0]),
            (router[:, :, 0:NG], router_c[0].rearrange("(k p) n -> p k n", p=P)),
            (router[:, :, NG:], router_f[0].rearrange("(k p) n -> p k n", p=P)),
            (rbias[:, 0:NG], router_c_b[0].partition_broadcast(P)),
            (rbias[:, NG:], router_f_b[0].partition_broadcast(P)),
            (kcache, cache_k[0, 0].rearrange("s h d -> s (h d)")),
            (vcache, cache_v[0, 0].rearrange("s h d -> s (h d)")),
        ]
        for z in range(2):
            small += [(w0v[:, z, :], col(w0[0, z])), (a0v[:, z, :], col(a0[0, z]))]

        with nc.Block() as block:
            @block.sync
            def _(sp):
                for n, (src, w) in enumerate(chunk_src):
                    if n >= 3:
                        sp.wait_ge(ring_used, n - 2)
                    sp.dma_start(ring[:, n % 3, :, 0:w], src.rearrange("(k p) n -> p k n", p=P)).then_inc(ld_ring[n % 3], 16)
                    if n == 1:
                        for tt in range(NTT):
                            src_x = x_prompt[0] if tt == 0 else x_sample[0, (tt - 1) * P:tt * P, :]
                            sp.dma_start(xs[:, tt, :], src_x).then_inc(ld_x, 16)
                sp.wait_ge(shift_ok, NET)
                sp.wait_ge(kv_ok, NTT)
                sp.dma_start(new_cache_v[0, 0].rearrange("s h d -> s (h d)"), qkv[:, 0, D_ATTN + D_KV:]).then_inc(st_cv, 16)
                sp.wait_ge(st_cv, 16)

            @block.gpsimd
            def _(pool):
                pool.memset(lorabd, 0.0).then_inc(lora_zero, 1)
                pool.memset(raw, 0.0).then_inc(raw_zero, 1)

            @block.scalar
            def _(act):
                for i, v in enumerate((c_ctx, c[0])):
                    act.dma_start(cond[:, 0, :, i], v.rearrange("(k p) -> p k", p=P), allow_slow_non_contiguous=True).then_inc(ld_cond, 16)
                act.dma_start(const, consts).then_inc(ld_const, 16)
                for j in range(4):
                    act.dma_start(bmod2[0:2, j, :], b_mod[0, 512 * j:512 * (j + 1)].partition_broadcast(2)).then_inc(ld_bg, 16)
                act.dma_start(g1row[0:2, :], norm1_g[0].partition_broadcast(2)).then_inc(ld_bg, 16)
                act.wait_ge(ld_cond, 32)
                act.activation(cond[:, 1], cond[:, 0], ACT.Sigmoid).then_inc(cond_sig, 1)
                for dst, src in small:
                    act.dma_start(dst, src, allow_slow_non_contiguous=True).then_inc(ld_small, 16)
                act.wait_ge(lora_zero, 1)
                for z in range(2):
                    act.dma_start(lorabd[32 * z:32 * z + 32, z, :], w_lora_up[0, z]).then_inc(ld_small, 16)
                    act.dma_start(lorabd[64 + 32 * z:96 + 32 * z, 2 + z, :], a_lora_up[0, z]).then_inc(ld_small, 16)
                act.wait_ge(ld_x, 16 * NTT)
                ch = Chain(act, act1)
                for tt in range(NTT):
                    ch(act.activation(junk[:, tt % 2, :], xs[:, tt, :], ACT.Square, accum_out=ssq[:, tt:tt + 1]))
                act.wait_ge(var_ok, 1)
                act.activation(rstd, ssq, ACT.Sqrt).then_inc(std_ok, 1)
                n = 0
                for j in range(4):
                    for cc in range(2):
                        act.wait_ge(bc_mm, n + 1)
                        dst = (shift1 if j < 2 else gain1)[:, cc, 512 * (j % 2):512 * (j % 2 + 1)]
                        act.activation(dst, ps[:, 4 + n % 4, :], ACT.Copy).then_inc(bc_ok, 1)
                        n += 1
                for tt in range(NTT):
                    act.wait_ge(hT_mm, tt + 1)
                    b = 2 * (tt % 2)
                    act.activation(hT[:, :, tt * P:(tt + 1) * P],
                                   ps[:, b:b + 2, :].rearrange("p b (k t) -> p (b k) t", t=P), ACT.Copy).then_inc(hT_ok, 1)
                for tt in range(NTT):
                    act.wait_ge(qkv_mm, 2 * tt + 1)
                    act.activation(qkv[:, tt, 0:512], ps[:, 4 + 2 * (tt % 2), :], ACT.Copy).then_inc(q_ok, 1)
                act.wait_ge(ld_small, 16 * (len(small) + 4))
                act.wait_ge(raw_zero, 1)
                for e in range(NET):
                    m = P if e < NET - 1 else GATE_LORA
                    act.wait_ge(rw_mm, e + 1)
                    if e >= 2:
                        act.wait_ge(shift_ok, e - 1)
                    if e == 0:
                        act.wait_ge(mu_ready, 1)
                    act.activation(raw[0:m, e % 2, 1:129], ps[0:m, 2 + e % 2, 0:T_CTX], ACT.Copy)
                    act.activation(raw[0:m, e % 2, 130:642], ps[0:m, e % 2, :], ACT.Copy)
                    act.activation(rws[0:m, e, 0:T_CTX], ps[0:m, 2 + e % 2, 0:T_CTX], ACT.Copy, scale=mu_c0[0:m, e:e + 1])
                    act.activation(rws[0:m, e, T_CTX:], ps[0:m, e % 2, :], ACT.Copy, scale=mu_c0[0:m, e:e + 1]).then_inc(raw_ok, 1)

            @block.vector
            def _(dve):
                ch = Chain(dve, dve1)
                dve.wait_ge(cond_sig, 1)
                dve.tensor_tensor(cond2, cond[:, 1], cond[:, 0], ALU.mult).then_inc(cond_ready, 1)
                dve.wait_ge(ld_small, 16 * (len(small) + 4))
                ch(dve.memset(mu_c0, 1.0))
                for z in range(2):
                    for m, lo, hi in ((P, 0, NET - 1), (GATE_LORA, NET - 1, NET)):
                        ins = dve.tensor_tensor(mu_c0[0:m, lo:hi], mu_c0[0:m, lo:hi], mu[0:m, z, lo:hi], ALU.subtract)
                        ch(ins) if z == 0 or lo == 0 else ins.then_inc(mu_ready, 1)
                ch(dve.tensor_scalar(ka1v, kav, -1.0, 1.0, ALU.mult, ALU.add))
                dve.wait_ge(act1, NTT)
                dve.tensor_scalar(ssq, ssq, 1.0 / D, EPS, ALU.mult, ALU.add).then_inc(var_ok, 1)
                dve.wait_ge(std_ok, 1)
                ch(dve.reciprocal(rstd, rstd))
                dve.wait_ge(ld_bg, 16 * 5)
                for j in range(4):
                    dve.wait_ge(modrow_mm, j + 1)
                    row = modrow[0:2, j % 2, :]
                    if j >= 2:
                        dve.wait_ge(bc_mm, 2 * (j - 1))
                    if j < 2:
                        dve.tensor_tensor(row, ps[0:2, j, :], bmod2[0:2, j, :], ALU.add).then_inc(modrow_ok, 1)
                    else:
                        ch(dve.tensor_tensor(row, ps[0:2, j, :], bmod2[0:2, j, :], ALU.add))
                        dve.scalar_tensor_tensor(row, row, 1.0, g1row[0:2, 512 * (j - 2):512 * (j - 1)],
                                                 ALU.add, ALU.mult).then_inc(modrow_ok, 1)
                dve.wait_ge(bc_ok, 8)
                for tt in range(NTT):
                    cc = 0 if tt == 0 else 1
                    if tt >= 2:
                        dve.wait_ge(hT_mm, tt - 1)
                    ch(dve.scalar_tensor_tensor(htmp[:, tt % 2, :], xs[:, tt, :], rstd[:, tt:tt + 1], gain1[:, cc, :],
                                                ALU.mult, ALU.mult))
                    dve.tensor_tensor(htmp[:, tt % 2, :], htmp[:, tt % 2, :], shift1[:, cc, :], ALU.add).then_inc(h_ok, 1)
                for tt in range(NTT):
                    dve.wait_ge(qkv_mm, 2 * tt + 2)
                    dve.tensor_copy(qkv[:, tt, 512:768], ps[:, 5 + 2 * (tt % 2), 0:256]).then_inc(kv_ok, 1)
                for e in range(NET):
                    m = P if e < NET - 1 else GATE_LORA
                    dve.wait_ge(raw_ok, e + 1)
                    r_, o = raw[0:m, e % 2, :], rws[0:m, e, :]
                    for k, off in ((0, 0), (1, 2)):
                        for (a, b), base in (((0, T_CTX), 0), ((T_CTX, T), T_CTX + 1)):
                            ins = dve.scalar_tensor_tensor(o[:, a:b], r_[:, base + off:base + off + b - a],
                                                           mu[0:m, k, e:e + 1], o[:, a:b], ALU.mult, ALU.add)
                            if k == 1 and a:
                                ins.then_inc(shift_ok, 1)
                            else:
                                ch(ins)

            @block.tensor
            def _(pe):
                pe.wait_ge(cond_ready, 1)
                for j in range(4):
                    pe.wait_ge(ld_ring[j % 3], 16 * (j // 3 + 1))
                    for k in range(KT):
                        mm = pe.matmul(ps[0:2, j, :], cond2[:, k, :], ring[:, j % 3, k, :], start=(k == 0), stop=(k == KT - 1))
                    mm.then_inc(modrow_mm, 1)
                    pe.wait_ge(modrow_mm, j + 1)
                    pe.nop().then_inc(ring_used, 1)
                pe.wait_ge(ld_const, 16)
                n = 0
                for j in range(4):
                    pe.wait_ge(modrow_ok, j + 1)
                    for cc in range(2):
                        if n >= 4:
                            pe.wait_ge(bc_ok, n - 3)
                        pe.matmul(ps[:, 4 + n % 4, :], sel[0:2, cc, :], modrow[0:2, j % 2, :], start=True, stop=True).then_inc(bc_mm, 1)
                        n += 1
                for tt in range(NTT):
                    pe.wait_ge(h_ok, tt + 1)
                    if tt >= 2:
                        pe.wait_ge(hT_ok, tt - 1)
                    b = 2 * (tt % 2)
                    for k in range(KT):
                        mm = pe.transpose(ps[:, b + k // 4, (k % 4) * P:(k % 4 + 1) * P], htmp[:, tt % 2, k * P:(k + 1) * P], ident)
                    mm.then_inc(hT_mm, 1)
                pe.wait_ge(hT_ok, NTT)
                pe.wait_ge(bc_ok, 8)
                pe.wait_ge(ld_ring[1], 32)
                pe.wait_ge(ld_ring[2], 32)
                for tt in range(NTT):
                    b = 4 + 2 * (tt % 2)
                    if tt >= 2:
                        pe.wait_ge(q_ok, tt - 1)
                        pe.wait_ge(kv_ok, tt - 1)
                    for half, w in ((0, 512), (1, 256)):
                        for k in range(KT):
                            mm = pe.matmul(ps[:, b + half, 0:w], hT[:, k, tt * P:(tt + 1) * P],
                                           ring[:, (4 + half) % 3, k, 0:w], start=(k == 0), stop=(k == KT - 1))
                        mm.then_inc(qkv_mm, 1)
                pe.wait_ge(qkv_mm, 2 * NTT)
                pe.nop().then_inc(ring_used, 1)
                pe.nop().then_inc(ring_used, 1)
                for e in range(NET):
                    n = 6 + e // 4
                    if e % 4 == 0:
                        pe.wait_ge(ld_ring[n % 3], 16 * (n // 3 + 1))
                    m = P if e < NET - 1 else GATE_LORA
                    if e >= 2:
                        pe.wait_ge(raw_ok, e - 1)
                    for lo, hi, b in ((T_CTX, T, e % 2), (0, T_CTX, 2 + e % 2)):
                        for k in range(KT):
                            mm = pe.matmul(ps[0:m, b, 0:hi - lo], ring[:, n % 3, k, (e % 4) * P:(e % 4) * P + m],
                                           hT[:, k, lo:hi], start=(k == 0), stop=(k == KT - 1))
                    mm.then_inc(rw_mm, 1)
                    if e % 4 == 3:
                        pe.wait_ge(rw_mm, e + 1)
                        pe.nop().then_inc(ring_used, 1)

        at = R
        sq = view(at, NTT, 640)
        qn = view(at + 3200, NTT, 640); at += 6400
        qT = view(at, 4, T); at += 4 * T
        kT = view(at, T + PAST); at += T + PAST
        prob = view(at, 2, 640); at += 1280
        probT = view(at, 2, 640); at += 1280
        rot1 = view(at, 640); rot2 = view(at + 640, 640); at += 1280
        attn = view(at, NTT, 512); at += NTT * 512
        attnT = view(at, 4, T); at += 4 * T
        hss, hrs = view(at, NTT, 10), view(at + 50, NTT, 10); at += 100
        negmax, rsum, rinv = view(at, 40), view(at + 40, 40), view(at + 80, 40); at += 120
        zrow = view(at, D); at += D
        SC = HD ** -0.5

        z_set, z_filled = sem("z_set"), sem("z_filled")
        units = [(tt, h) for tt in range(NTT) for h in range(NQ)]
        (sq_ok, hss_ok, hstd_ok, qn_ok, kc_out, tp_mm, tp_ok, s_mm, max_ok, exp_ok, pt_mm, pt_ok, pv_mm, at_ok,
         aT_mm, aT_ok, st_aT, dve2, act2) = (sem(n) for n in (
             "sq_ok", "hss_ok", "hstd_ok", "qn_ok", "kc_out", "tp_mm", "tp_ok", "s_mm", "max_ok", "exp_ok", "pt_mm",
             "pt_ok", "pv_mm", "at_ok", "aT_mm", "aT_ok", "st_aT", "dve2", "act2"))

        with nc.Block() as block:
            @block.sync
            def _(sp):
                sp.wait_ge(z_set, 1)
                sp.dma_start(xg_d.rearrange("(n p) d -> p n d", p=P), zrow.unsqueeze(1).to_broadcast([P, NT + 1, D])).then_inc(z_filled, 16)
                sp.dma_start(yg_d[MIN_TILES * P:].rearrange("(n p) d -> p n d", p=P), zrow.unsqueeze(1).to_broadcast([P, NT - MIN_TILES, D])).then_inc(z_filled, 16)
                sp.wait_ge(qn_ok, 1)
                sp.dma_start(new_cache_k[0, 0].rearrange("s h d -> s (h d)"), qn[:, 0, 512:640]).then_inc(kc_out, 16)
                sp.wait_ge(aT_ok, NTT)
                sp.dma_start(attn_d, attnT.rearrange("p a t -> p (a t)")).then_inc(st_aT, 16)
                sp.wait_ge(kc_out, 16)
                sp.wait_ge(st_aT, 16)
                sp.wait_ge(z_filled, 32)

            @block.gpsimd
            def _(pool):
                pool.memset(zrow, 0.0).then_inc(z_set, 1)

            @block.vector
            def _(dve):
                ch = Chain(dve, dve2)
                dve.wait_ge(sq_ok, 1)
                ch(dve.tensor_reduce(hss.rearrange("p a b -> p (a b)"), sq.rearrange("p a (h d) -> p (a h) d", d=HD), AX.X, ALU.add))
                dve.tensor_scalar(hss, hss, 1.0 / HD, EPS, ALU.mult, ALU.add).then_inc(hss_ok, 1)
                dve.wait_ge(hstd_ok, 1)
                ch(dve.reciprocal(hrs, hrs))
                for tt in range(NTT):
                    x = qn[:, tt, :]
                    xh = x.rearrange("p (h d) -> p h d", d=HD)
                    q_out = x[:, 0:512].rearrange("p (j g d) -> p g j d", g=2, d=HD)
                    r1 = rot1.rearrange("p (h d) -> p h d", d=HD)
                    ch(dve.tensor_tensor(r1, qkv[:, tt, 0:640].rearrange("p (h d) -> p h d", d=HD),
                                         hrs[:, tt, :].unsqueeze(2).to_broadcast([P, 10, HD]), ALU.mult))
                    if tt == 0:
                        for g in range(2):
                            dve.tensor_tensor(q_out[:, g], r1[:, 4 * g:4 * g + 4], gq.unsqueeze(1).to_broadcast([P, 4, HD]), ALU.mult)
                        dve.tensor_tensor(xh[:, 8:10], r1[:, 8:10], gk.unsqueeze(1).to_broadcast([P, 2, HD]), ALU.mult).then_inc(qn_ok, 1)
                        dve.wait_ge(qn_ok, 1)
                        continue
                    dve.tensor_tensor(xh[:, 0:8], r1[:, 0:8], gq.unsqueeze(1).to_broadcast([P, 8, HD]), ALU.mult)
                    ch(dve.tensor_tensor(xh[:, 8:10], r1[:, 8:10], gk.unsqueeze(1).to_broadcast([P, 2, HD]), ALU.mult))
                    cosb = rope_c[:, tt - 1, :].unsqueeze(1).to_broadcast([P, 10, HD])
                    dve.tensor_tensor(r1, xh, cosb, ALU.mult)
                    x4 = x.rearrange("p (h a d) -> p h a d", a=4, d=16)
                    o4 = rot2.rearrange("p (h a d) -> p h a d", a=4, d=16)
                    s4 = rope_s[:, tt - 1, :].rearrange("p (a d) -> p a d", a=4)
                    for k in range(4):
                        ins = dve.tensor_tensor(o4[:, :, k, :], x4[:, :, k ^ 1, :],
                                                s4[:, k, :].unsqueeze(1).to_broadcast([P, 10, 16]), ALU.mult)
                    ch(ins)
                    r2 = rot2.rearrange("p (h d) -> p h d", d=HD)
                    for g in range(2):
                        dve.tensor_tensor(q_out[:, g], r1[:, 4 * g:4 * g + 4], r2[:, 4 * g:4 * g + 4], ALU.add)
                    dve.tensor_tensor(xh[:, 8:10], r1[:, 8:10], r2[:, 8:10], ALU.add).then_inc(qn_ok, 1)
                    dve.wait_ge(qn_ok, tt + 1)
                for n, (tt, h) in enumerate(units + [(0, 0)] * 2):
                    if n < len(units):
                        w = P if tt == 0 else 640
                        dve.wait_ge(s_mm, n + 1)
                        s_ = ps[:, 2 * (n % 2):2 * (n % 2) + 2, :].rearrange("p b n -> p (b n)")[:, 0:w]
                        ch(dve.reduce_max(negmax[:, n:n + 1], s_, AX.X))
                        dve.tensor_scalar(negmax[:, n:n + 1], negmax[:, n:n + 1], -SC, None, ALU.mult).then_inc(max_ok, 1)
                    if n >= 2:
                        m = n - 2
                        ch(dve.reciprocal(rinv[:, m:m + 1], rsum[:, m:m + 1]))
                        dve.wait_ge(pv_mm, m + 1)
                        tm, hm = units[m]
                        dve.tensor_scalar(attn[:, tm, hm * HD:(hm + 1) * HD], ps[:, 6 + m % 2, 0:HD], rinv[:, m:m + 1],
                                          None, ALU.mult).then_inc(at_ok, 1)

            @block.scalar
            def _(act):
                act.activation(sq, qkv[:, :, 0:640], ACT.Square).then_inc(sq_ok, 1)
                act.wait_ge(hss_ok, 1)
                act.activation(hrs, hss, ACT.Sqrt).then_inc(hstd_ok, 1)
                act.wait_ge(tp_mm, 1)
                act.activation(kT[:, T:T + PAST], ps[:, 0, 0:P], ACT.Copy).then_inc(tp_ok, 1)
                for tt in range(NTT):
                    act.wait_ge(tp_mm, tt + 2)
                    b = 2 * ((tt + 1) % 2)
                    act.activation(kT[:, tt * P:(tt + 1) * P], ps[:, b, 0:P], ACT.Copy)
                    act.activation(qT[:, :, tt * P:(tt + 1) * P], ps[:, b + 1, :].rearrange("p (j t) -> p j t", t=P),
                                   ACT.Copy).then_inc(tp_ok, 1)
                for n, (tt, h) in enumerate(units + [(0, 0)]):
                    if n < len(units):
                        w = P if tt == 0 else 640
                        act.wait_ge(max_ok, n + 1)
                        if n >= 2:
                            act.wait_ge(pt_mm, n - 1)
                        s_ = ps[:, 2 * (n % 2):2 * (n % 2) + 2, :].rearrange("p b n -> p (b n)")[:, 0:w]
                        act.activation(prob[:, n % 2, 0:w], s_, ACT.Exp, bias=negmax[:, n:n + 1], scale=SC,
                                       accum_out=rsum[:, n:n + 1]).then_inc(exp_ok, 1)
                    if n >= 1:
                        m = n - 1
                        wm = P if units[m][0] == 0 else 640
                        act.wait_ge(pt_mm, m + 1)
                        if m >= 2:
                            act.wait_ge(pv_mm, m - 1)
                        act.activation(probT[:, m % 2, 0:wm],
                                       ps[:, 4:6, :].rearrange("p b n -> p (b n)")[:, 0:wm], ACT.Copy).then_inc(pt_ok, 1)
                for tt in range(NTT):
                    act.wait_ge(aT_mm, tt + 1)
                    act.activation(attnT[:, :, tt * P:(tt + 1) * P], ps[:, tt % 2, :].rearrange("p (j t) -> p j t", t=P),
                                   ACT.Copy).then_inc(aT_ok, 1)

            @block.tensor
            def _(pe):
                pe.transpose(ps[:, 0, 0:P], kcache, ident).then_inc(tp_mm, 1)
                for tt in range(NTT):
                    pe.wait_ge(qn_ok, tt + 1)
                    if tt >= 1:
                        pe.wait_ge(tp_ok, tt)
                    b = 2 * ((tt + 1) % 2)
                    pe.transpose(ps[:, b, 0:P], qn[:, tt, 512:640], ident)
                    for j in range(4):
                        mm = pe.transpose(ps[:, b + 1, j * P:(j + 1) * P],
                                          qn[:, tt, j * P:(j + 1) * P], ident)
                    mm.then_inc(tp_mm, 1)
                pe.wait_ge(tp_ok, NTT + 1)

                def scores(n):
                    tt, h = units[n]
                    if n >= 2:
                        pe.wait_ge(exp_ok, n - 1)
                    r = slice(64 * (h // 4), 64 * (h // 4) + 64)
                    q_ = qT[r, h % 4, tt * P:(tt + 1) * P]
                    b = 2 * (n % 2)
                    if tt == 0:
                        mm = pe.matmul(ps[:, b, 0:P], q_, kT[r, 0:P], start=True, stop=True)
                    else:
                        pe.matmul(ps[:, b, :], q_, kT[r, P:T], start=True, stop=True)
                        mm = pe.matmul(ps[:, b + 1, 0:P], q_, kT[r, T:T + PAST], start=True, stop=True)
                    mm.then_inc(s_mm, 1)

                def transposes(n):
                    tt, h = units[n]
                    pe.wait_ge(exp_ok, n + 1)
                    if n >= 1:
                        pe.wait_ge(pt_ok, n)
                    for y in range(1 if tt == 0 else 5):
                        mm = pe.transpose(ps[:, 4 + y // 4, (y % 4) * P:(y % 4 + 1) * P], prob[:, n % 2, y * P:(y + 1) * P], ident)
                    mm.then_inc(pt_mm, 1)

                def values(n):
                    tt, h = units[n]
                    pe.wait_ge(pt_ok, n + 1)
                    if n >= 2:
                        pe.wait_ge(at_ok, n - 1)
                    v0 = D_ATTN + D_KV + HD * (h // 4)
                    if tt == 0:
                        vs = [qkv[:, 0, v0:v0 + HD]]
                    else:
                        vs = [qkv[:, y, v0:v0 + HD] for y in range(1, NTT)] + [vcache[:, HD * (h // 4):HD * (h // 4) + HD]]
                    for y, v_ in enumerate(vs):
                        mm = pe.matmul(ps[:, 6 + n % 2, 0:HD], probT[:, n % 2, y * P:(y + 1) * P], v_,
                                       start=(y == 0), stop=(y == len(vs) - 1))
                    mm.then_inc(pv_mm, 1)

                scores(0)
                for n in range(len(units)):
                    if n + 1 < len(units):
                        scores(n + 1)
                    transposes(n)
                    if n >= 1:
                        values(n - 1)
                values(len(units) - 1)
                for tt in range(NTT):
                    pe.wait_ge(at_ok, min(len(units), NQ * (tt + 1)))
                    if tt >= 2:
                        pe.wait_ge(aT_ok, tt - 1)
                    for j in range(4):
                        mm = pe.transpose(ps[:, tt % 2, j * P:(j + 1) * P], attn[:, tt, j * P:(j + 1) * P], ident)
                    mm.then_inc(aT_mm, 1)

        chm = view(R, 2, 4, NC4, T)
        bonus = view(R + 8 * NC4 * T, NC4, T)
        at = R + 9 * NC4 * T
        t_x, t_rk, e_0, em_0, ei_0 = (view(at + i * T, T) for i in range(5)); at += 5 * T
        t_b, t_cs, t_csm = (view(at + 2 * i * T, 2, T) for i in range(3)); at += 6 * T
        ksq = view(at, NC4, T)
        assert at + NC4 * T <= 53000, at
        t_e, t_em, t_ei = ((a_, ksq[:, i]) for i, a_ in enumerate((e_0, em_0, ei_0)))
        A_, R_, B_, K_ = range(4)
        vt = view(CB + NET * T, NCH, NC4, C)
        vt_mm, vt_ok = sem("vt_mm"), sem("vt_ok")
        lora_in, gate_in = rws[:, 12, :], rws[:, 13, :]
        (lact_ok, wl_mm, sig_ok, kk_ok, ksq_ok, n_mm, n_ok, nstd_ok, rk_ok, bo_mm, bo_ok, cs_ok, csm_ok, exps_ok,
         ops_done, st_bo, dve3, act3) = (sem(n) for n in (
             "lact_ok", "wl_mm", "sig_ok", "kk_ok", "ksq_ok", "n_mm", "n_ok", "nstd_ok", "rk_ok", "bo_mm", "bo_ok",
             "cs_ok", "csm_ok", "exps_ok", "ops_done", "st_bo", "dve3", "act3"))
        kd_ok, b_used, pool3 = sem("kd_ok"), sem("b_used"), sem("pool3")

        def two_banks(b, m=P):
            return ps[0:m, b:b + 2, 0:T // 2]

        def halves(v):
            return v.rearrange("p (b n) -> p b n", b=2)

        with nc.Block() as block:
            @block.sync
            def _(sp):
                sp.wait_ge(bo_ok, NC4)
                sp.dma_start(bonus_d, bonus.rearrange("p a t -> p (a t)")).then_inc(st_bo, 16)
                sp.wait_ge(st_bo, 16)

            @block.gpsimd
            def _(pool):
                ch = Chain(pool, pool3)
                pool.wait_ge(sig_ok, 4 * NC4)
                pool.wait_ge(kk_ok, 1)
                n = 0
                for c4 in range(NC4):
                    for z in (1, 0):
                        rate = chm[:, z, K_, c4, :]
                        if n >= 2:
                            pool.wait_ge(b_used, n - 1)
                        ch(pool.tensor_tensor(t_b[:, n % 2], chm[:, 0, A_, c4, :], rate, ALU.mult))
                        ch(pool.tensor_scalar(rate, rate, kav[:, c4:c4 + 1], ka1v[:, c4:c4 + 1], ALU.mult, ALU.add))
                        pool.tensor_tensor(rate, rate, rws[:, 4 + c4, :], ALU.mult).then_inc(kd_ok, 1)
                        n += 1

            @block.tensor
            def _(pe):
                pe.wait_ge(lact_ok, 1)
                n = 0
                for c4 in range(NC4):
                    for j in range(4):
                        if n >= 2:
                            pe.wait_ge(sig_ok, n - 1)
                        for hf in range(2):
                            mm = pe.matmul(ps[:, 2 * (n % 2) + hf, 0:T // 2], lorabd[:, j, c4 * P:(c4 + 1) * P],
                                           lora_in[:, hf * T // 2:(hf + 1) * T // 2], start=True, stop=True)
                        mm.then_inc(wl_mm, 1)
                        n += 1
                for ch_i in range(NCH):
                    b = 2 * (ch_i % 2)
                    if ch_i >= 2:
                        pe.wait_ge(vt_ok, ch_i - 1)
                    else:
                        pe.wait_ge(sig_ok, 4 * NC4)
                    for j in range(NC4):
                        for p in range(2):
                            r_ = slice(64 * p, 64 * p + 64)
                            mm = pe.matmul(ps[r_, b, j * C:(j + 1) * C], rws[r_, 8 + j, ch_i * C:(ch_i + 1) * C], istack[r_, :], start=True, stop=True)
                    mm.then_inc(vt_mm, 1)
                for c4 in range(NC4):
                    pe.wait_ge(ksq_ok, c4 + 1)
                    if c4 >= 1:
                        pe.wait_ge(n_ok, c4)
                    for hf in range(2):
                        mm = pe.matmul(ps[:, 4 + hf, 0:T // 2], blockones, ksq[:, c4, hf * T // 2:(hf + 1) * T // 2], start=True, stop=True)
                    mm.then_inc(n_mm, 1)
                    pe.wait_ge(rk_ok, c4 + 1)
                    if c4 >= 1:
                        pe.wait_ge(bo_ok, c4)
                    for hf in range(2):
                        mm = pe.matmul(ps[:, 6 + hf, 0:T // 2], blockones, t_rk[:, hf * T // 2:(hf + 1) * T // 2], start=True, stop=True)
                    mm.then_inc(bo_mm, 1)

            @block.scalar
            def _(act):
                ch = Chain(act, act3)
                ch(act.activation(gate_in[0:GATE_LORA, :], gate_in[0:GATE_LORA, :], ACT.Sigmoid))
                act.activation(lora_in[0:64, :], lora_in[0:64, :], ACT.Tanh).then_inc(lact_ok, 1)
                n = 0
                for c4 in range(NC4):
                    for j in range(4):
                        act.wait_ge(wl_mm, n + 1)
                        dst = chm[:, j % 2, B_ if j < 2 else K_, c4, :]
                        bias = (w0v if j < 2 else a0v)[:, j % 2, c4:c4 + 1]
                        act.activation(halves(dst), two_banks(2 * (n % 2)), ACT.Sigmoid, bias=bias).then_inc(sig_ok, 1)
                        n += 1
                for ch_i in range(NCH):
                    act.wait_ge(vt_mm, ch_i + 1)
                    act.activation(vt[:, ch_i], ps[:, 2 * (ch_i % 2), 0:NC4 * C].rearrange("p (j n) -> p j n", j=NC4), ACT.Copy).then_inc(vt_ok, 1)
                act.wait_ge(n_ok, NC4)
                act.activation(ksq, ksq, ACT.Sqrt).then_inc(nstd_ok, 1)
                n = 0
                for c4 in range(NC4):
                    for z in (1, 0):
                        act.wait_ge(csm_ok, n + 1)
                        b = n % 2
                        if n >= 2:
                            act.wait_ge(ops_done, n - 1)
                        act.activation(t_e[b], t_cs[:, b], ACT.Exp, scale=-DS)
                        act.activation(t_em[b], t_csm[:, b], ACT.Exp, scale=-DS)
                        act.activation(t_ei[b], t_cs[:, b], ACT.Exp, scale=DS)
                        last = C - 1 if z == 0 else 0
                        act.activation(pc_all[:, z, c4, :], t_cs[:, b].rearrange("p (c t) -> p c t", t=C)[:, :, last],
                                       ACT.Exp, scale=-DS).then_inc(exps_ok, 1)
                        n += 1

            @block.vector
            def _(dve):
                ch = Chain(dve, dve3)
                for c4 in range(NC4):
                    kk = chm[:, 0, A_, c4, :]
                    ch(dve.tensor_scalar(kk, rws[:, 4 + c4, :], kkv[:, c4:c4 + 1], None, ALU.mult))
                    dve.tensor_tensor(ksq[:, c4, :], kk, kk, ALU.mult).then_inc(ksq_ok, 1)
                    if c4 >= 1:
                        dve.wait_ge(bo_mm, c4)
                    dve.scalar_tensor_tensor(t_rk, rws[:, c4, :], rkv[:, c4:c4 + 1], rws[:, 4 + c4, :], ALU.mult, ALU.mult).then_inc(rk_ok, 1)
                    dve.wait_ge(n_mm, c4 + 1)
                    dve.tensor_scalar(halves(ksq[:, c4, :]), two_banks(4), 1e-12, None, ALU.add).then_inc(n_ok, 1)
                    dve.wait_ge(bo_mm, c4 + 1)
                    dve.tensor_tensor(halves(bonus[:, c4, :]), two_banks(6), halves(rws[:, 8 + c4, :]), ALU.mult).then_inc(bo_ok, 1)
                dve.wait_ge(nstd_ok, 1)
                ch(dve.reciprocal(ksq, ksq))
                ch(dve.tensor_tensor(chm[:, 0, A_], chm[:, 0, A_], ksq, ALU.mult))
                dve.nop().then_inc(kk_ok, 1)
                dve.wait_ge(sig_ok, 4 * NC4)

                def sums(n):
                    c4, z, b = n // 2, 1 - n % 2, n % 2
                    sig, cs = chm[:, z, B_, c4, :], t_cs[:, b]
                    if n >= 2:
                        dve.wait_ge(exps_ok, n - 1)
                    if z == 0:
                        ch(dve.tensor_tensor_scan(cs, scanmask, sig, 0.0, ALU.mult, ALU.add))
                    else:
                        ch(dve.tensor_tensor_scan(t_x, scanmask, sig, 0.0, ALU.mult, ALU.add))
                        x3 = t_x.rearrange("p (c t) -> p c t", t=C)
                        ch(dve.tensor_tensor(cs.rearrange("p (c t) -> p c t", t=C),
                                             x3[:, :, C - 1:C].to_broadcast([P, NCH, C]), x3, ALU.subtract))
                        ch(dve.tensor_tensor(cs, cs, sig, ALU.add))
                    dve.tensor_tensor(t_csm[:, b], cs, sig, ALU.subtract).then_inc(csm_ok, 1)

                sums(0)
                for n in range(2 * NC4):
                    if n + 1 < 2 * NC4:
                        sums(n + 1)
                    c4, z, b = n // 2, 1 - n % 2, n % 2
                    rate = chm[:, z, K_, c4, :]
                    dve.wait_ge(exps_ok, n + 1)
                    dve.tensor_tensor(chm[:, z, R_, c4, :], rws[:, c4, :], t_e[b], ALU.mult)
                    dve.wait_ge(kd_ok, n + 1)
                    dve.tensor_tensor(chm[:, z, B_, c4, :], t_b[:, b], t_ei[b], ALU.mult).then_inc(b_used, 1)
                    dve.tensor_tensor(rate, rate, t_ei[b], ALU.mult)
                    if n >= 1:
                        dve.wait_ge(ops_done, n)
                    dve.tensor_tensor(chm[:, z, A_, c4, :], chm[:, 0, A_, c4, :], t_em[b], ALU.mult).then_inc(ops_done, 1)

        with nc.Block() as block:
            @block.gpsimd
            def _(pool):
                nc.clear_and_free_semaphores(phase_sems)

        at = CB
        bdin = view(at, 2, 2, NC4, P); at += 4 * NC4 * P
        ari = view(at, 2, NC4, 3, C); at += 6 * NC4 * C
        ars = view(at, 2, 2, NC4, C); at += 4 * NC4 * C
        assert at <= CB + 8 * T
        at = CB + NET * T + NCH * NC4 * C
        S = view(at, 2, NC4, C); at += 2 * NC4 * C
        Vc = view(at, 2, NC4, C); at += 2 * NC4 * C
        assert at <= R
        at = R + 8 * NC4 * T
        HC = 2 * NC4 * C
        LTc = view(at, 2, NC4, C); at += HC
        Lm = view(at, 2, 2, NC4, C); at += 2 * HC
        MTc, RKc, RBc = (view(at + i * HC, 2, NC4, C) for i in range(3)); at += 3 * HC
        yacc = view(at, NCH, NC4, C); at += NCH * NC4 * C
        Ktc, Btc, Xc, XTc, Zc, Uc, stage_in, stage_out = (view(at + i * HC, 2, NC4, C) for i in range(8)); at += 8 * HC
        RHc = Zc
        assert at <= 53000, at
        N_CTX = T_CTX // C
        spans = ((0, N_CTX, 0), (T_CTX, T_LAT // C, N_CTX))
        LV = LEVELS - 1

        def sems(*names):
            return [[sem(f"{n}_{d}") for d in ("fwd", "bwd")] for n in names]

        (bdg, bds, lm_ok, xt1_ok, gB, gK, lg_mm4, w_mm, xt_mm, xq_mm, rhs_mm, u_mm, y_mm, sn_mm, lt_ok, rb_ok, rk_ok,
         vc_ok, x1_tmp, x1_ok, z_ok, xt_ok, xc_ok, rh_ok, uc_ok, y_ok, s_add, s_ok) = sems(
            "bd_bk", "ar_seq", "lm_ok", "xt1_ok", "gram_b", "gram_k", "gram_l", "w_mm", "xt_mm", "xq_mm", "rhs_mm", "u_mm",
            "y_mm", "sn_mm", "lt_ok", "rb_ok", "rk_ok", "vc_ok", "x1_tmp", "x1_ok", "z_ok", "xt_ok", "xc_ok", "rh_ok",
            "uc_ok", "y_ok", "s_add", "s_ok")
        zero4, half_ok, ld_state, st_state, so_mm, si_mm, so_ok, si_ok = (sem(n) for n in (
            "zero4", "half_ok", "ld_state", "st_state", "state_out_mm", "state_in_mm", "state_out_ok", "state_in_ok"))
        settled = sem("settled")
        GB, GK = 0, 2
        W4, X4 = 4, 6

        def start_counts(eng, *pairs):
            for pair in pairs:
                for one in pair:
                    eng.nop().then_inc(one, 1)

        def settle(eng):
            eng.nop().then_inc(settled, 1)

        def quarter(bank):
            return ps[:, bank, 0:NC4 * C].rearrange("p (j n) -> p j n", j=NC4)

        def gram(bank, k):
            return ps[:, bank:bank + 2, 0:6 * C].rearrange("p b (j n) -> p b j n", j=2)[:, :, :, k * C:(k + 1) * C]

        def by2(v):
            return v.rearrange("p (b j) n -> p b j n", b=2)

        def rows(v, p):
            return v[64 * p:64 * p + 64]

        def chunks(eng, i, t0, n, size=C):
            f = t0 // C
            return eng.snap((i + f) * size), eng.snap((i * -1 + (f + n - 1)) * size)

        with nc.Block() as block:
            @block.sync
            def _(sp):
                for z in range(2):
                    for p in range(2):
                        sp.dma_start(rows(stage_in[:, z], p), state_rwkv[0, 0, z].rearrange("(j p) v k -> p v j k", p=2)[p]).then_inc(ld_state, 16)
                sp.wait_ge(so_ok, 1)
                for z in range(2):
                    for p in range(2):
                        sp.dma_start(new_state[0, 0, z].rearrange("(j p) v k -> p v j k", p=2)[p], rows(stage_out[:, z], p)).then_inc(st_state, 16)
                sp.wait_ge(st_state, 64)

            @block.gpsimd
            def _(pool):
                pool.memset(bdin, 0.0).then_inc(zero4, 1)
                pool.tensor_copy(ari[:, :, :, 2, :].rearrange("p z j n -> p (z j) n"), istack.unsqueeze(1).to_broadcast([P, 2 * NC4, C])).then_inc(zero4, 1)
                pool.memset(S, 0.0).then_inc(zero4, 1)
                pool.memset(yacc, 0.0).then_inc(zero4, 1)
                pool.wait_ge(zero4, 4)
                start_counts(pool, bdg, bds, lm_ok, xt1_ok)
                for t0, n, s0 in spans:
                    with pool.Fori(0, n) as i:
                        s = i + s0
                        tok = chunks(pool, i, t0, n)
                        for z in range(2):
                            pool.wait_ge(gK[z], s + 1)
                            pool.wait_ge(lg_mm4[z], s + 1)
                            for p in range(2):
                                settle(pool)
                                r_ = slice(64 * p, 64 * p + 64)
                                ins = pool.tensor_copy(bdin[r_, z, :, :, 64 * p:64 * p + 64].rearrange("p a j t -> p (a j) t"),
                                                       chm[r_, z, 2:4, :, bass.ds(tok[z], C)].rearrange("p a j t -> p (a j) t"))
                                ins.then_inc(half_ok, 1)
                                pool.wait_ge(half_ok, s * 4 + 2 * z + p + 1)
                            settle(pool)
                            for a in range(2):
                                ins = pool.tensor_copy(ari[:, z, :, a, :], chm[:, z, a, :, bass.ds(tok[z], C)])
                            ins.then_inc(bdg[z], 1)

                        def level(z, l):
                            pool.wait_ge(lt_ok[z], s + 2)
                            pool.wait_ge(w_mm[z], s * LV + max(l - 2, 0) + 1)
                            pool.tensor_tensor(Lm[:, z, l % 2], LTc[:, z], levels[:, z, l].unsqueeze(1).to_broadcast([P, NC4, C]),
                                               ALU.mult).then_inc(lm_ok[z], 1)

                        for z in range(2):
                            pool.wait_ge(lt_ok[z], s + 2)
                            pool.tensor_tensor(XTc[:, z], LTc[:, z], levels[:, z, 0].unsqueeze(1).to_broadcast([P, NC4, C]), ALU.mult).then_inc(xt1_ok[z], 1)
                            level(z, 1)
                            pool.wait_ge(xt1_ok[z], s * 2 + 2)
                            pool.tensor_tensor(XTc[:, z], XTc[:, z], istack.unsqueeze(1).to_broadcast([P, NC4, C]), ALU.add).then_inc(xt1_ok[z], 1)
                        for l in range(2, LEVELS):
                            for z in range(2):
                                level(z, l)
                                if l == 2:
                                    pool.wait_ge(y_mm[z], s + 1)
                                    settle(pool)
                                    pool.tensor_copy(ars[:, z].rearrange("p a j t -> p (a j) t"),
                                                     chm[:, z, 0:2, :, bass.ds(tok[z], C)].rearrange("p a j t -> p (a j) t")).then_inc(bds[z], 1)

            @block.tensor
            def _(pe):
                pe.wait_ge(zero4, 4)
                start_counts(pe, gB, gK, lg_mm4, w_mm, xt_mm, xq_mm, rhs_mm, u_mm, y_mm, sn_mm)

                def product(bank, z, terms):
                    settle(pe)
                    for j in range(NC4):
                        for k, (lhs, rhs) in enumerate(terms):
                            for p in range(2):
                                r_ = rhs if rhs is istack else rhs[:, j]
                                mm = pe.matmul(ps[64 * p:64 * p + 64, bank + z, j * C:(j + 1) * C], rows(lhs[:, j], p), rows(r_, p),
                                               start=(k == 0), stop=(k == len(terms) - 1))
                    return mm

                for t0, n, s0 in spans:
                    if t0:
                        for z in range(2):
                            pe.wait_ge(s_ok[z], s0 + 1)
                            mm = product(W4, z, [(S[:, z], istack)])
                        mm.then_inc(so_mm, 1)
                        pe.wait_ge(ld_state, 64)
                        pe.wait_ge(y_ok[0], s0 + 1)
                        pe.wait_ge(y_ok[1], s0 + 1)
                        for z in range(2):
                            mm = product(X4, z, [(stage_in[:, z], istack)])
                        mm.then_inc(si_mm, 1)
                        pe.wait_ge(so_ok, 1)
                        pe.wait_ge(si_ok, 1)
                    with pe.Fori(0, n) as i:
                        s = i + s0
                        for z in range(2):
                            prev = s if z == 0 else s + 1
                            pe.wait_ge(bdg[z], s + 2)
                            pe.wait_ge(rb_ok[1 - z], prev + 1)
                            for bank, a, free, done in ((GB, 0, rb_ok, gB), (GK, 1, rk_ok, gK)):
                                pe.wait_ge(free[1 - z], prev + 1)
                                for j in range(NC4):
                                    mm = pe.matmul(ps[:, bank + j // 2, (j % 2) * 3 * C:(j % 2 + 1) * 3 * C], bdin[:, z, a, j],
                                                   ari[:, z, j].rearrange("p a n -> p (a n)"), start=True, stop=True)
                                mm.then_inc(done[z], 1)
                            pe.wait_ge(s_ok[z], s + 1)
                            settle(pe)
                            for j in range(NC4):
                                for p in range(2):
                                    mm = pe.matmul(ps[64 * p:64 * p + 64, W4 + z, j * C:(j + 1) * C], rows(ari[:, z, j, 0], p),
                                                   rows(bdin[:, z, 0, j], p)[:, 64 * p:64 * p + 64], start=True, stop=True)
                            mm.then_inc(lg_mm4[z], 1)
                        for l in range(1, LEVELS):
                            for z in range(2):
                                pe.wait_ge(lm_ok[z], s * LV + l + 1)
                                if l == 1:
                                    pe.wait_ge(x1_ok[z], s + 2)
                                else:
                                    pe.wait_ge(xt_ok[z], s * LV + l)
                                    pe.wait_ge(xc_ok[z], s * (LV - 1) + l)
                                product(W4, z, [(Lm[:, z, l % 2], Xc[:, z])]).then_inc(w_mm[z], 1)
                            for z in range(2):
                                pe.wait_ge(z_ok[z], s * LV + l + 1)
                                if l == 1:
                                    pe.wait_ge(xt1_ok[z], s * 2 + 3)
                                    pe.wait_ge(y_ok[z], s + 1)
                                if l < LEVELS - 1:
                                    product(X4, z, [(XTc[:, z], Zc[:, z])]).then_inc(xq_mm[z], 1)
                                product(W4, z, [(Zc[:, z], XTc[:, z])]).then_inc(xt_mm[z], 1)
                        for z in range(2):
                            pe.wait_ge(bds[z], s + 2)
                            pe.wait_ge(rk_ok[z], s + 2)
                            pe.wait_ge(vc_ok[z], s + 2)
                            pe.wait_ge(xc_ok[z], s * (LV - 1) + LV)
                            product(X4, z, [(ars[:, z, 0], S[:, z]), (MTc[:, z], Vc[:, z])]).then_inc(rhs_mm[z], 1)
                        for z in range(2):
                            pe.wait_ge(rh_ok[z], s + 2)
                            pe.wait_ge(xt_ok[z], s * LV + LV + 1)
                            product(W4, z, [(XTc[:, z], RHc[:, z])]).then_inc(u_mm[z], 1)
                        for z in range(2):
                            pe.wait_ge(uc_ok[z], s + 2)
                            product(X4, z, [(ars[:, z, 1], S[:, z]), (RKc[:, z], Vc[:, z]), (RBc[:, z], Uc[:, z])]).then_inc(y_mm[z], 1)
                            product(W4, z, [(Ktc[:, z], Vc[:, z]), (Btc[:, z], Uc[:, z])]).then_inc(sn_mm[z], 1)

            @block.scalar
            def _(act):
                act.wait_ge(zero4, 4)
                start_counts(act, vc_ok, xt_ok, uc_ok)
                for t0, n, s0 in spans:
                    if t0:
                        act.wait_ge(so_mm, 1)
                        act.activation(stage_out, ps[:, 4:6, 0:NC4 * C].rearrange("p z (j n) -> p z j n", j=NC4), ACT.Copy).then_inc(so_ok, 1)
                    with act.Fori(0, n) as i:
                        s = i + s0
                        chunk = chunks(act, i, t0, n, 1)
                        for z in range(2):
                            act.wait_ge(sn_mm[z], s + 1)
                            act.activation(Vc[:, z], vt[:, bass.ds(chunk[z], 1)].squeeze(1), ACT.Copy).then_inc(vc_ok[z], 1)
                        for l in range(1, LEVELS):
                            for z in range(2):
                                act.wait_ge(xt_mm[z], s * LV + l + 1)
                                act.activation(XTc[:, z], quarter(W4 + z), ACT.Copy).then_inc(xt_ok[z], 1)
                        for z in range(2):
                            act.wait_ge(u_mm[z], s + 2)
                            act.activation(Uc[:, z], quarter(W4 + z), ACT.Copy).then_inc(uc_ok[z], 1)

            @block.vector
            def _(dve):
                dve.wait_ge(zero4, 4)
                start_counts(dve, lt_ok, rb_ok, rk_ok, x1_tmp, x1_ok, z_ok, xc_ok, rh_ok, y_ok, s_add, s_ok)
                eye = istack.unsqueeze(1).to_broadcast([P, NC4, C])

                def masked(dst, src, m):
                    mb = m.unsqueeze(1).to_broadcast([P, 2, C])
                    for b in range(2):
                        ins = dve.tensor_tensor(by2(dst)[:, b], src[:, b], mb, ALU.mult)
                    return ins

                for t0, n, s0 in spans:
                    if t0:
                        dve.wait_ge(si_mm, 1)
                        dve.tensor_copy(S, ps[:, 6:8, 0:NC4 * C].rearrange("p z (j n) -> p z j n", j=NC4)).then_inc(si_ok, 1)
                    with dve.Fori(0, n) as i:
                        s = i + s0
                        chunk = chunks(dve, i, t0, n, 1)
                        for z in range(2):
                            dve.wait_ge(gB[z], s + 2)
                            dve.wait_ge(lm_ok[z], s * LV + 1)
                            dve.tensor_copy(by2(LTc[:, z]), gram(GB, 0)).then_inc(lt_ok[z], 1)
                            masked(RBc[:, z], gram(GB, 1), mnegincl[:, z])
                            dve.tensor_scalar(by2(Btc[:, z]), gram(GB, 2), -1.0, None, ALU.mult).then_inc(rb_ok[z], 1)
                            dve.wait_ge(gK[z], s + 2)
                            masked(MTc[:, z], gram(GK, 0), mstrict[:, z])
                            masked(RKc[:, z], gram(GK, 1), mincl[:, z])
                            dve.tensor_copy(by2(Ktc[:, z]), gram(GK, 2)).then_inc(rk_ok[z], 1)
                            dve.wait_ge(lg_mm4[z], s + 2)
                            dve.tensor_tensor(Xc[:, z], quarter(W4 + z), levels[:, 1 - z, 0].unsqueeze(1).to_broadcast([P, NC4, C]), ALU.mult).then_inc(x1_tmp[z], 1)
                            dve.wait_ge(x1_tmp[z], s + 2)
                            dve.tensor_tensor(Xc[:, z], Xc[:, z], eye, ALU.add).then_inc(x1_ok[z], 1)
                        for l in range(1, LEVELS):
                            for z in range(2):
                                dve.wait_ge(w_mm[z], s * LV + l + 1)
                                dve.tensor_tensor(Zc[:, z], quarter(W4 + z), eye, ALU.add).then_inc(z_ok[z], 1)
                            if l < LEVELS - 1:
                                for z in range(2):
                                    dve.wait_ge(xq_mm[z], s * (LV - 1) + l + 1)
                                    dve.tensor_copy(Xc[:, z], quarter(X4 + z)).then_inc(xc_ok[z], 1)
                        for z in range(2):
                            dve.wait_ge(rhs_mm[z], s + 2)
                            dve.tensor_copy(RHc[:, z], quarter(X4 + z)).then_inc(rh_ok[z], 1)
                        for z in range(2):
                            dve.wait_ge(y_mm[z], s + 2)
                            dve.wait_ge(y_ok[z], s + 1)
                            dve.wait_ge(y_ok[1 - z], s + 1 + z)
                            ya = yacc[:, bass.ds(chunk[z], 1)].squeeze(1)
                            dve.tensor_tensor(ya, ya, quarter(X4 + z), ALU.add).then_inc(y_ok[z], 1)
                            dve.wait_ge(sn_mm[z], s + 2)
                            dve.tensor_tensor(S[:, z], S[:, z], quarter(W4 + z), ALU.add).then_inc(s_add[z], 1)
                            dve.wait_ge(s_add[z], s + 2)
                            pc_ = pc_all[:, z, :, bass.ds(chunk[z], 1)].to_broadcast([P, NC4, C])
                            dve.tensor_tensor(S[:, z], S[:, z], pc_, ALU.mult).then_inc(s_ok[z], 1)

        catT = view(CB, 2 * NC4, T)
        h2T = catT
        bmodA, g2row = view(CB + 8 * T, 4, 512), view(CB + 8 * T + 2048, D)
        assert 8 * T + 2048 + D <= 13 * T
        bmodB = lorabd
        modrow2 = view(CB + NET * T + 2 * D, 2, 512)
        at = R
        bonus2 = view(at, NC4, T)
        yn = view(at + NC4 * T, NCH, NC4, C)
        h2 = view(at, NTT, D); at += NTT * D
        ring2 = view(at, 3, KT, 512); at += 3 * KT * 512
        gate1, shift2, gain2 = (view(at + i * 2 * D, 2, D) for i in range(3)); at += 6 * D
        XS = 53000 - NTT * D
        xs2 = view(XS, NTT, D)
        gate2 = view(XS - 2 * D, 2, D)
        assert at <= R + 8 * NC4 * T + 6 * HC and R + 8 * NC4 * T + 6 * HC + NCH * NC4 * C <= XS - 2 * D
        tmp5 = view(CB + NET * T, 2, D)
        free0 = _CONST["levels"][0] + 0
        lv = [free0]

        def small_view(*shape):
            v = view(lv[0], *shape)
            lv[0] += int(np.prod(shape))
            assert lv[0] <= _CONST["scanmask"][0]
            return v

        gmean, gvar = small_view(NCH * NC4), small_view(NCH * NC4)
        logits = small_view(NTT, NG + NE)
        mxc, m2c, gsum, m1f, m2f, e2 = (small_view(NTT) for _ in range(6))
        eqc, ghot, expc, lsel, eq1, hot1, l2, hot2 = (small_view(NTT, 4) for _ in range(8))
        prod = small_view(NTT, NE)
        E1, E2, Msum, posn = (small_view(NTT, NE) for _ in range(4))
        cnt, ntile, incl, base, one16 = (small_view(NE) for _ in range(5))
        cmp = small_view(NT, NE)
        eid_f = small_view(NT + 1)
        half_iota = small_view(NT // 2)

        chunk2 = [(w_mod[0][:, 512 * j:512 * (j + 1)]) for j in range(4, 12)] + [w_out[0][:, 0:512], w_out[0][:, 512:]]
        (ld_ring20, ld_ring21, ld_ring22, ld_in5, ld_rows5, used2, mr_mm, mr_ok, mb_mm, mb_ok, gm_ok, gsq_ok, gv_ok,
         gs_ok, yn_ok, yT_mm, g_mm, cat_ok, mix_mm, x2_ok, ss_ok, v2_ok, sd2_ok, h2_ok, h2T_mm, h2T_ok, lg_mm, lgs_ok,
         ec_ok, ex_ok, d2_ok, e2_ok, m_ok, rank_mm, slot_ok, scattered, dve5, act5) = (sem(n) for n in (
             "ld_ring2_0", "ld_ring2_1", "ld_ring2_2", "ld_in5", "ld_rows5", "used2", "mr_mm", "mr_ok", "mb_mm",
             "mb_ok", "gm_ok", "gsq_ok", "gv_ok", "gs_ok", "yn_ok", "yT_mm", "g_mm", "cat_ok", "mix_mm", "x2_ok",
             "ss_ok", "v2_ok", "sd2_ok", "h2_ok", "h2T_mm", "h2T_ok", "lg_mm", "lgs_ok", "ec_ok", "ex_ok", "d2_ok",
             "e2_ok", "m_ok", "rank_mm", "slot_ok", "scattered", "dve5", "act5"))
        ld_ring2 = [ld_ring20, ld_ring21, ld_ring22]
        mods2 = (gate1, shift2, gain2, gate2)

        with nc.Block() as block:
            @block.sync
            def _(sp):
                for n, src in enumerate(chunk2):
                    if n >= 3:
                        sp.wait_ge(used2, n - 2)
                    sp.dma_start(ring2[:, n % 3], src.rearrange("(k p) n -> p k n", p=P)).then_inc(ld_ring2[n % 3], 16)
                sp.wait_ge(slot_ok, 1)

            @block.gpsimd
            def _(pool):
                pool.wait_ge(slot_ok, 1)
                for tt in range(NTT):
                    for r in range(2):
                        pool.indirect_dma_start(
                            out=xg_d, out_offset=bass.IndirectOffsetOnAxis(ap=slot_i[:, r * NTT + tt:r * NTT + tt + 1], axis=0),
                            in_=h2[:, tt, :], in_offset=None).then_inc(scattered, 16)
                pool.wait_ge(scattered, 32 * NTT)

            @block.scalar
            def _(act):
                for j in range(4):
                    for rows_, first in ((bmodA, 4), (bmodB.rearrange("p a b -> p (a b)").rearrange("p (a b) -> p a b", a=4), 8)):
                        lo = 512 * (first + j)
                        act.dma_start(rows_[0:2, j, :], b_mod[0, lo:lo + 512].partition_broadcast(2)).then_inc(ld_rows5, 16)
                act.dma_start(g2row[0:2, :], norm2_g[0].partition_broadcast(2)).then_inc(ld_rows5, 16)
                act.dma_start(bonus2.rearrange("p a t -> p (a t)"), bonus_d).then_inc(ld_in5, 16)
                act.dma_start(catT[:, 0:NC4].rearrange("p a t -> p (a t)"), attn_d).then_inc(ld_in5, 16)
                for tt in range(NTT):
                    src_x = x_prompt[0] if tt == 0 else x_sample[0, (tt - 1) * P:tt * P, :]
                    act.dma_start(xs2[:, tt, :], src_x).then_inc(ld_in5, 16)
                act.wait_ge(gm_ok, 1)
                act.activation(yn, yacc, ACT.Square).then_inc(gsq_ok, 1)
                act.wait_ge(gv_ok, 1)
                act.activation(gvar, gvar, ACT.Sqrt).then_inc(gs_ok, 1)
                n = 0
                for j in range(8):
                    for cc in range(2):
                        act.wait_ge(mb_mm, n + 1)
                        act.activation(mods2[j // 2][:, cc, 512 * (j % 2):512 * (j % 2 + 1)], ps[:, 6 + n % 2, :], ACT.Copy).then_inc(mb_ok, 1)
                        n += 1
                ch = Chain(act, act5)
                for tt in range(NTT):
                    act.wait_ge(x2_ok, tt + 1)
                    ins = act.activation(ps[:, 4:6, :], xs2[:, tt, :].rearrange("p (b n) -> p b n", b=2), ACT.Square, accum_out=ssq[:, tt:tt + 1])
                    ins.then_inc(ss_ok, 1)
                    act.wait_ge(ss_ok, tt + 1)
                act.wait_ge(v2_ok, 1)
                act.activation(rstd, ssq, ACT.Sqrt).then_inc(sd2_ok, 1)
                for tt in range(NTT):
                    act.wait_ge(h2T_mm, tt + 1)
                    b = 2 * (tt % 2)
                    act.activation(h2T[:, :, tt * P:(tt + 1) * P],
                                   ps[:, b:b + 2, :].rearrange("p b (k t) -> p (b k) t", t=P), ACT.Copy).then_inc(h2T_ok, 1)
                act.wait_ge(ec_ok, 1)
                act.activation(expc, expc, ACT.Exp).then_inc(ex_ok, 1)
                act.wait_ge(d2_ok, 1)
                act.activation(e2, e2, ACT.Exp).then_inc(e2_ok, 1)

            @block.tensor
            def _(pe):
                def mod_chunk(j):
                    pe.wait_ge(ld_ring2[j % 3], 16 * (j // 3 + 1))
                    if j >= 2:
                        pe.wait_ge(mr_ok, j - 1)
                    for k in range(KT):
                        mm = pe.matmul(ps[0:2, 4 + j % 2, :], cond2[:, k, :], ring2[:, j % 3, k, :], start=(k == 0), stop=(k == KT - 1))
                    mm.then_inc(mr_mm, 1)
                    pe.wait_ge(mr_mm, j + 1)
                    pe.nop().then_inc(used2, 1)

                def mod_rows(j):
                    pe.wait_ge(mr_ok, j + 1)
                    for cc in range(2):
                        n = 2 * j + cc
                        if n >= 2:
                            pe.wait_ge(mb_ok, n - 1)
                        pe.matmul(ps[:, 6 + n % 2, :], sel[0:2, cc, :], modrow2[0:2, j % 2, :], start=True, stop=True).then_inc(mb_mm, 1)

                def turn(c4):
                    if c4 >= 1:
                        pe.wait_ge(cat_ok, c4)
                    for ch_i in range(NCH):
                        for p in range(2):
                            mm = pe.matmul(ps[64 * p:64 * p + 64, ch_i // 5, (ch_i % 5) * C:(ch_i % 5 + 1) * C],
                                           rows(yn[:, ch_i, c4], p), rows(istack, p), start=True, stop=True)
                    mm.then_inc(yT_mm, 1)
                    for hf in range(2):
                        mm = pe.matmul(ps[:, 2 + hf, 0:T // 2], glora[0:GATE_LORA, c4 * P:(c4 + 1) * P],
                                       gate_in[0:GATE_LORA, hf * T // 2:(hf + 1) * T // 2], start=True, stop=True)
                    mm.then_inc(g_mm, 1)

                mod_chunk(0)
                for j in range(1, 8):
                    mod_chunk(j)
                    mod_rows(j - 1)
                    if j == 2:
                        pe.wait_ge(yn_ok, 1)
                    if 2 <= j < 6:
                        turn(j - 2)
                mod_rows(7)
                pe.wait_ge(cat_ok, NC4)
                pe.wait_ge(ld_in5, 16 * 7)
                pe.wait_ge(ld_ring2[8 % 3], 16 * 3)
                pe.wait_ge(ld_ring2[9 % 3], 16 * 4)
                for tt in range(NTT):
                    b = 2 * (tt % 2)
                    if tt >= 2:
                        pe.wait_ge(x2_ok, tt - 1)
                    for half in range(2):
                        for k in range(KT):
                            mm = pe.matmul(ps[:, b + half, :], catT[:, k, tt * P:(tt + 1) * P], ring2[:, (8 + half) % 3, k, :],
                                           start=(k == 0), stop=(k == KT - 1))
                    mm.then_inc(mix_mm, 1)
                for tt in range(NTT):
                    pe.wait_ge(h2_ok, tt + 1)
                    b = 2 * (tt % 2)
                    if tt >= 2:
                        pe.wait_ge(h2T_ok, tt - 1)
                    for k in range(KT):
                        mm = pe.transpose(ps[:, b + k // 4, (k % 4) * P:(k % 4 + 1) * P], h2[:, tt, k * P:(k + 1) * P], ident)
                    mm.then_inc(h2T_mm, 1)
                pe.wait_ge(h2T_ok, NTT)
                for tt in range(NTT):
                    for k in range(KT):
                        mm = pe.matmul(ps[:, 6, tt * 32:tt * 32 + NG + NE], h2T[:, k, tt * P:(tt + 1) * P], router[:, k, :],
                                       start=(k == 0), stop=(k == KT - 1))
                mm.then_inc(lg_mm, 1)
                pe.wait_ge(m_ok, 1)
                for tt in range(NTT + 1):
                    out = ps[:, 7, tt * NE:(tt + 1) * NE]
                    for t2 in range(min(tt, NTT)):
                        mm = pe.matmul(out, ones, Msum[:, t2, :], start=(t2 == 0), stop=(tt == NTT and t2 == NTT - 1))
                    if tt < NTT:
                        mm = pe.matmul(out, stricttri, Msum[:, tt, :], start=(tt == 0), stop=True)
                mm.then_inc(rank_mm, 1)

            @block.vector
            def _(dve):
                ch = Chain(dve, dve5)

                def bc(v, n):
                    return v.unsqueeze(2).to_broadcast([P, v.shape[1], n])

                ya = yacc.rearrange("p a b c -> p (a b) c")
                yb = yn.rearrange("p a b c -> p (a b) c")
                ch(dve.tensor_reduce(gmean, ya, AX.X, ALU.add))
                ch(dve.tensor_scalar(gmean, gmean, 1.0 / C, None, ALU.mult))
                dve.tensor_tensor(ya, ya, bc(gmean, C), ALU.subtract).then_inc(gm_ok, 1)
                dve.wait_ge(gsq_ok, 1)
                ch(dve.tensor_reduce(gvar, yb, AX.X, ALU.add))
                dve.tensor_scalar(gvar, gvar, 1.0 / C, GN_EPS, ALU.mult, ALU.add).then_inc(gv_ok, 1)
                dve.wait_ge(gs_ok, 1)
                ch(dve.reciprocal(gvar, gvar))
                dve.tensor_tensor(yb, ya, bc(gvar, C), ALU.mult).then_inc(yn_ok, 1)
                dve.wait_ge(ld_rows5, 16 * 9)
                dve.wait_ge(ld_in5, 16 * 7)
                bB = bmodB.rearrange("p a b -> p (a b)").rearrange("p (a b) -> p a b", a=4)

                def mod_row(j):
                    dve.wait_ge(mr_mm, j + 1)
                    if j >= 2:
                        dve.wait_ge(mb_mm, 2 * (j - 1))
                    row = modrow2[0:2, j % 2, :]
                    bm = (bmodA if j < 4 else bB)[0:2, j % 4, :]
                    if j // 2 != 2:
                        dve.tensor_tensor(row, ps[0:2, 4 + j % 2, :], bm, ALU.add).then_inc(mr_ok, 1)
                    else:
                        ch(dve.tensor_tensor(row, ps[0:2, 4 + j % 2, :], bm, ALU.add))
                        dve.scalar_tensor_tensor(row, row, 1.0, g2row[0:2, 512 * (j - 4):512 * (j - 3)], ALU.add, ALU.mult).then_inc(mr_ok, 1)

                def cat(c4):
                    t5 = tmp5.rearrange("p a b -> p (a b)")[:, 0:T]
                    dve.wait_ge(yT_mm, c4 + 1)
                    ch(dve.tensor_scalar(halves(t5), two_banks(0), lngv[:, c4:c4 + 1], lnbv[:, c4:c4 + 1], ALU.mult, ALU.add))
                    ch(dve.tensor_tensor(t5, t5, bonus2[:, c4, :], ALU.add))
                    dve.wait_ge(g_mm, c4 + 1)
                    dve.tensor_tensor(halves(catT[:, NC4 + c4, :]), halves(t5), two_banks(2), ALU.mult).then_inc(cat_ok, 1)

                for j in range(8):
                    mod_row(j)
                    if 2 <= j < 6:
                        cat(j - 2)
                dve.wait_ge(mb_ok, 16)
                for tt in range(NTT):
                    cc = 0 if tt == 0 else 1
                    dve.wait_ge(mix_mm, tt + 1)
                    b = 2 * (tt % 2)
                    ch(dve.tensor_tensor(tmp5[:, tt % 2, :].rearrange("p (b n) -> p b n", b=2), ps[:, b:b + 2, :],
                                         gate1[:, cc, :].rearrange("p (b n) -> p b n", b=2), ALU.mult))
                    dve.tensor_tensor(xs2[:, tt, :], xs2[:, tt, :], tmp5[:, tt % 2, :], ALU.add).then_inc(x2_ok, 1)
                dve.wait_ge(ss_ok, NTT)
                dve.tensor_scalar(ssq, ssq, 1.0 / D, EPS, ALU.mult, ALU.add).then_inc(v2_ok, 1)
                dve.wait_ge(sd2_ok, 1)
                ch(dve.reciprocal(rstd, rstd))
                for tt in range(NTT):
                    cc = 0 if tt == 0 else 1
                    ch(dve.scalar_tensor_tensor(h2[:, tt, :], xs2[:, tt, :], rstd[:, tt:tt + 1], gain2[:, cc, :], ALU.mult, ALU.mult))
                    dve.tensor_tensor(h2[:, tt, :], h2[:, tt, :], shift2[:, cc, :], ALU.add).then_inc(h2_ok, 1)
                prio_b = cst("prio").unsqueeze(1).to_broadcast([P, NTT, 4])

                def first_max(hot, eq, vals, mx, m2):
                    ch(dve.tensor_reduce(mx, vals, AX.X, ALU.max))
                    ch(dve.tensor_tensor(eq, vals, bc(mx, 4), ALU.is_equal))
                    ch(dve.tensor_tensor(eq, eq, prio_b, ALU.mult))
                    ch(dve.tensor_reduce(m2, eq, AX.X, ALU.max))
                    ch(dve.tensor_tensor(hot, eq, bc(m2, 4), ALU.is_equal))

                ch(dve.memset(one16, 1.0))
                dve.wait_ge(lg_mm, 1)
                ch(dve.tensor_tensor(logits, ps[:, 6, 0:NTT * 32].rearrange("p (t n) -> p t n", n=32)[:, :, 0:NG + NE],
                                     rbias.unsqueeze(1).to_broadcast([P, NTT, NG + NE]), ALU.add))
                lc = logits[:, :, 0:NG]
                first_max(ghot, eqc, lc, mxc, m2c)
                dve.tensor_tensor(expc, lc, bc(mxc, 4), ALU.subtract).then_inc(ec_ok, 1)
                dve.wait_ge(ex_ok, 1)
                ch(dve.tensor_reduce(gsum, expc, AX.X, ALU.add))
                p4 = prod.rearrange("p t (g e) -> p t g e", g=NG)
                for g in range(NG):
                    ins = dve.tensor_tensor(p4[:, :, g, :], logits[:, :, NG + 4 * g:NG + 4 * g + 4],
                                            ghot[:, :, g:g + 1].to_broadcast([P, NTT, 4]), ALU.mult)
                ch(ins)
                ch(dve.tensor_reduce(lsel, prod.rearrange("p t (g e) -> p t e g", g=NG), AX.X, ALU.add))
                first_max(hot1, eq1, lsel, m1f, m2c)
                ch(dve.scalar_tensor_tensor(l2, hot1, -BIG, lsel, ALU.mult, ALU.add))
                first_max(hot2, eq1, l2, m2f, m2c)
                dve.tensor_tensor(e2, m2f, m1f, ALU.subtract).then_inc(d2_ok, 1)
                dve.wait_ge(e2_ok, 1)
                ch(dve.tensor_scalar(m1f, e2, 1.0, None, ALU.add))
                ch(dve.tensor_tensor(m1f, m1f, gsum, ALU.mult))
                ch(dve.reciprocal(wsel[:, 0, :], m1f))
                ch(dve.tensor_tensor(wsel[:, 1, :], wsel[:, 0, :], e2, ALU.mult))
                for E_, hot in ((E1, hot1), (E2, hot2)):
                    for g in range(NG):
                        ins = dve.tensor_tensor(E_[:, :, 4 * g:4 * g + 4], hot, ghot[:, :, g:g + 1].to_broadcast([P, NTT, 4]), ALU.mult)
                ch(ins)
                dve.tensor_tensor(Msum, E1, E2, ALU.add).then_inc(m_ok, 1)
                dve.wait_ge(rank_mm, 1)
                ch(dve.tensor_copy(cnt, ps[:, 7, NTT * NE:(NTT + 1) * NE]))
                ch(dve.tensor_scalar(ntile, cnt, 0.0, None, ALU.is_gt))
                for j in range(1, NTT):
                    ch(dve.scalar_tensor_tensor(ntile, cnt, float(P * j), ntile, ALU.is_gt, ALU.add))
                ch(dve.tensor_tensor_scan(incl, one16, ntile, 0.0, ALU.mult, ALU.add))
                ch(dve.tensor_tensor(base, incl, ntile, ALU.subtract))
                ch(dve.tensor_scalar(base, base, float(P), None, ALU.mult))
                ch(dve.tensor_tensor(posn, ps[:, 7, 0:NTT * NE].rearrange("p (t e) -> p t e", e=NE),
                                     base.unsqueeze(1).to_broadcast([P, NTT, NE]), ALU.add))
                for r, E_ in enumerate((E1, E2)):
                    ch(dve.tensor_tensor(prod, E_, posn, ALU.mult))
                    ch(dve.tensor_reduce(slot_f[:, r, :], prod, AX.X, ALU.add))
                ch(dve.tensor_copy(slot_i[:, :], slot_f.rearrange("p r t -> p (r t)")))
                ch(dve.tensor_tensor(cmp, incl.unsqueeze(1).to_broadcast([P, NT, NE]), cst("tile_iota").unsqueeze(2).to_broadcast([P, NT, NE]), ALU.is_le))
                ch(dve.tensor_reduce(eid_f[:, 0:NT], cmp, AX.X, ALU.add))
                ch(dve.tensor_scalar(eid_f[:, 0:NT], eid_f[:, 0:NT], float(NE - 1), None, ALU.min))
                ch(dve.tensor_scalar(half_iota, cst("tile_iota")[:, 1::2], incl[:, NE - 1:NE], None, ALU.is_lt))
                ch(dve.tensor_reduce(eid_f[:, NT:NT + 1], half_iota, AX.X, ALU.add))
                dve.tensor_copy(eid_i[:, :], eid_f).then_inc(slot_ok, 1)

        at = CB
        wg, wu = view(at, 2, KT, FE), view(at + 2 * KT * FE, 2, KT, FE); at += 4 * KT * FE
        wd = view(at, 2, 4, D); at += 8 * D
        xg = view(at, 2, D); at += 2 * D
        xgT = view(at, KT, P); at += KT * P
        sg, hid = view(at, FE), view(at + FE, FE); at += 2 * FE
        hidT = view(at, 4, P); at += 4 * P
        yo = view(at, 2, D); at += 2 * D
        assert at <= XS - 2 * D
        ld_xg, ld_gu, ld_wd, y_st = ([sem(f"{n}_{u}") for u in range(2)] for n in ("ld_xg", "ld_gu", "ld_wd", "y_stored"))
        (xgT_mm, xgT_ok, g6_mm, u6_mm, sg_ok, hsg_ok, hid_ok, hT6_mm, hT6_ok, y6_mm, yo_a, yo_v) = (sem(n) for n in (
            "xgT_mm", "xgT_ok", "gate_mm", "up_mm", "sig6_ok", "gsig_ok", "hid_ok", "hidT_mm", "hidT_ok", "down_mm",
            "yo_act", "yo_dve"))
        all_stored = sem("all_stored")
        GA, UP, XT0, HT, Y0 = 0, 1, 2, 4, 5
        PAIRS = (NT - 1) // 2

        def pairs_used(eng):
            return eng.value_load(eid_i[0:1, NT:NT + 1], min_val=MIN_TILES // 2, max_val=PAIRS)

        with nc.Block() as block:
            @block.sync
            def _(sp):
                def load(i, u):
                    e = sp.value_load(eid_i[0:1, bass.ds(i, 1)] if not isinstance(i, int) else eid_i[0:1, i:i + 1], min_val=0, max_val=NE - 1)
                    sp.dma_start(wg[:, u], exp_gate[0][bass.ds(e, 1)].squeeze(0).rearrange("(k p) n -> p k n", p=P)).then_inc(ld_gu[u], 16)
                    sp.dma_start(wu[:, u], exp_up[0][bass.ds(e, 1)].squeeze(0).rearrange("(k p) n -> p k n", p=P)).then_inc(ld_gu[u], 16)
                    return e

                def load_down(e, u):
                    sp.dma_start(wd[:, u], exp_down[0][bass.ds(e, 1)].squeeze(0).rearrange("(k p) n -> p k n", p=P)).then_inc(ld_wd[u], 16)

                def load_x(i, u):
                    sp.dma_start(xg[:, u], xg_d[bass.ds(i * P, P), :]).then_inc(ld_xg[u], 16)

                pairs = pairs_used(sp)
                load_x(0, 0)
                load_down(load(0, 0), 0)
                load_x(1, 1)
                with sp.Fori(0, PAIRS) as j:
                    with sp.If(j < pairs):
                        for u in (1, 0):
                            i = j * 2 + (2 - u)
                            sp.wait_ge(u6_mm, i)
                            e = load(i, u)
                            sp.wait_ge(xgT_mm, i + 1)
                            load_x(i + 1, 1 - u)
                            sp.wait_ge(y6_mm, i)
                            load_down(e, u)

            @block.tensor
            def _(pe):
                def x_turn(i, u, n):
                    pe.wait_ge(ld_xg[u], n)
                    for k in range(KT):
                        mm = pe.transpose(ps[:, XT0 + k // 4, (k % 4) * P:(k % 4 + 1) * P], xg[:, u, k * P:(k + 1) * P], ident)
                    mm.then_inc(xgT_mm, 1)

                def gate_up(i, u, n):
                    pe.wait_ge(ld_gu[u], n)
                    pe.wait_ge(xgT_ok, i + 1)
                    for w, b, s_ in ((wg, GA, g6_mm), (wu, UP, u6_mm)):
                        for k in range(KT):
                            mm = pe.matmul(ps[:, b, :], xgT[:, k, :], w[:, u, k, :], start=(k == 0), stop=(k == KT - 1))
                        mm.then_inc(s_, 1)

                def h_turn(i):
                    pe.wait_ge(hid_ok, i + 1)
                    for k in range(4):
                        mm = pe.transpose(ps[:, HT, k * P:(k + 1) * P], hid[:, k * P:(k + 1) * P], ident)
                    mm.then_inc(hT6_mm, 1)

                def down(i, u, n):
                    pe.wait_ge(ld_wd[u], n)
                    pe.wait_ge(hT6_ok, i + 1)
                    for half in range(2):
                        for k in range(4):
                            mm = pe.matmul(ps[:, Y0 + half, :], hidT[:, k, :], wd[:, u, k, half * 512:(half + 1) * 512],
                                           start=(k == 0), stop=(k == 3))
                    mm.then_inc(y6_mm, 1)

                pairs = pairs_used(pe)
                for one in (xgT_mm, u6_mm, y6_mm):
                    pe.nop().then_inc(one, 1)
                x_turn(0, 0, 16)
                gate_up(0, 0, 32)
                x_turn(1, 1, 16)
                with pe.Fori(0, PAIRS) as j:
                    with pe.If(j < pairs):
                        for u in (1, 0):
                            i = j * 2 + (2 - u)
                            h_turn(i - 1)
                            gate_up(i, u, (j * 32) + (32 if u else 64))
                            x_turn(i + 1, 1 - u, (j * 16) + 32)
                            pe.wait_ge(yo_a, i)
                            pe.wait_ge(yo_v, i)
                            down(i - 1, 1 - u, (j * 16) + 16)
                last = pe.snap(pairs * 2)
                h_turn(last)
                pe.wait_ge(yo_a, last + 1)
                pe.wait_ge(yo_v, last + 1)
                down(last, 0, pairs * 16 + 16)

            @block.scalar
            def _(act):
                def sigmoid(i):
                    act.wait_ge(g6_mm, i + 1)
                    act.activation(sg, ps[:, GA, :], ACT.Sigmoid).then_inc(sg_ok, 1)

                def x_out(i):
                    act.wait_ge(xgT_mm, i + 2)
                    act.activation(xgT, ps[:, XT0:XT0 + 2, :].rearrange("p b (k t) -> p (b k) t", t=P), ACT.Copy).then_inc(xgT_ok, 1)

                def h_out(i):
                    act.wait_ge(hT6_mm, i + 1)
                    act.activation(hidT, ps[:, HT, :].rearrange("p (k t) -> p k t", t=P), ACT.Copy).then_inc(hT6_ok, 1)

                def y_out(i, u, n):
                    act.wait_ge(y6_mm, i + 2)
                    act.wait_ge(y_st[u], n)
                    act.activation(yo[:, u, 0:512], ps[:, Y0, :], ACT.Copy).then_inc(yo_a, 1)
                    act.wait_ge(yo_a, i + 2)
                    act.wait_ge(yo_v, i + 2)
                    act.dma_start(yg_d[bass.ds(i * P, P), :], yo[:, u]).then_inc(y_st[u], 16)

                pairs = pairs_used(act)
                act.nop().then_inc(yo_a, 1)
                act.nop().then_inc(y_st[0], 16)
                act.nop().then_inc(y_st[1], 16)
                x_out(0)
                sigmoid(0)
                x_out(1)
                with act.Fori(0, PAIRS) as j:
                    with act.If(j < pairs):
                        for u in (1, 0):
                            i = j * 2 + (2 - u)
                            h_out(i - 1)
                            sigmoid(i)
                            x_out(i + 1)
                            y_out(i - 1, 1 - u, j * 16 + 16)
                last = act.snap(pairs * 2)
                h_out(last)
                y_out(last, 0, pairs * 16 + 16)
                act.wait_ge(y_st[0], pairs * 16 + 32)
                act.wait_ge(y_st[1], pairs * 16 + 16)
                act.nop().then_inc(all_stored, 1)

            @block.vector
            def _(dve):
                def hidden(i):
                    dve.wait_ge(sg_ok, i + 1)
                    dve.tensor_tensor(sg, sg, ps[:, GA, :], ALU.mult).then_inc(hsg_ok, 1)
                    dve.wait_ge(hsg_ok, i + 1)
                    dve.wait_ge(u6_mm, i + 2)
                    dve.tensor_tensor(hid, sg, ps[:, UP, :], ALU.mult).then_inc(hid_ok, 1)

                def y_out(i, u, n):
                    dve.wait_ge(y6_mm, i + 2)
                    dve.wait_ge(y_st[u], n)
                    dve.tensor_copy(yo[:, u, 512:], ps[:, Y0 + 1, :]).then_inc(yo_v, 1)

                pairs = pairs_used(dve)
                dve.nop().then_inc(yo_v, 1)
                hidden(0)
                with dve.Fori(0, PAIRS) as j:
                    with dve.If(j < pairs):
                        for u in (1, 0):
                            i = j * 2 + (2 - u)
                            hidden(i)
                            y_out(i - 1, 1 - u, j * 16 + 16)
                y_out(pairs * 2, 0, pairs * 16 + 16)

        yA, yB = view(CB, NTT, D), view(CB + NTT * D, NTT, D)
        got, y7, st7, dve7 = [sem(f"gathered_{tt}") for tt in range(NTT)], sem("y7"), sem("st7"), sem("dve7")

        with nc.Block() as block:
            @block.gpsimd
            def _(pool):
                for tt in range(NTT):
                    for r, dst in enumerate((yA, yB)):
                        pool.indirect_dma_start(
                            out=dst[:, tt, :], out_offset=None, in_=yg_d,
                            in_offset=bass.IndirectOffsetOnAxis(ap=slot_i[:, r * NTT + tt:r * NTT + tt + 1], axis=0)).then_inc(got[tt], 16)

            @block.vector
            def _(dve):
                ch = Chain(dve, dve7)
                for tt in range(NTT):
                    cc = 0 if tt == 0 else 1
                    dve.wait_ge(got[tt], 32)
                    ch(dve.tensor_scalar(yA[:, tt, :], yA[:, tt, :], wsel[:, 0, tt:tt + 1], None, ALU.mult))
                    ch(dve.scalar_tensor_tensor(yA[:, tt, :], yB[:, tt, :], wsel[:, 1, tt:tt + 1], yA[:, tt, :], ALU.mult, ALU.add))
                    ch(dve.tensor_tensor(yA[:, tt, :], yA[:, tt, :], gate2[:, cc, :], ALU.mult))
                    dve.tensor_tensor(yA[:, tt, :], yA[:, tt, :], xs2[:, tt, :], ALU.add).then_inc(y7, 1)

            @block.sync
            def _(sp):
                for tt in range(NTT):
                    sp.wait_ge(y7, tt + 1)
                    dst = y_prompt[0] if tt == 0 else y_sample[0, (tt - 1) * P:tt * P, :]
                    sp.dma_start(dst, yA[:, tt, :]).then_inc(st7, 16)
                sp.wait_ge(st7, 16 * NTT)


_INS = ['x_prompt', 'x_sample', 'cache_k', 'cache_v', 'state_rwkv', 'c', 'c_ctx', 'w_mod', 'b_mod', 'norm1_g',
        'norm2_g', 'w_in', 'mu_shift', 'q_norm_g', 'k_norm_g', 'w0', 'w_lora_up', 'a0', 'a_lora_up', 'g_lora_up',
        'k_k', 'k_a', 'r_k', 'ln_x_g', 'ln_x_b', 'w_out', 'router_c', 'router_c_b', 'router_f', 'router_f_b',
        'exp_gate', 'exp_up', 'exp_down']
_OUTS = [((1, T_CTX, D), 'float32'), ((1, T_LAT, D), 'float32'), ((1, 1, T_CTX, NKV, HD), 'float32'),
         ((1, 1, T_CTX, NKV, HD), 'float32'), ((1, 1, 2, 8, HD, HD), 'float32')]


def kernel(**inputs):
    import numpy as _np
    import concourse.bacc as _bacc
    from concourse import mybir as _mybir
    from concourse.bass_utils import run_bass_kernel_spmd as _run

    nc = _bacc.Bacc("TRN2", target_bir_lowering=False, num_devices=1)
    arrays, args = {}, []
    for name in _INS + ['consts']:
        a = const_table() if name == 'consts' else _np.ascontiguousarray(inputs[name])
        arrays[f"in_{name}_dram"] = a
        args.append(nc.dram_tensor(f"in_{name}_dram", a.shape, _mybir.dt.from_np(a.dtype), kind="ExternalInput").ap())
    for i, (shape, dtype) in enumerate(_OUTS):
        dt = _mybir.dt.from_np(_np.dtype(dtype))
        args.append(nc.dram_tensor(f"out_{i}_dram", shape, dt, kind="ExternalOutput").ap())
    build(nc, *args)
    r = _run(nc, [arrays], core_ids=[0])
    return tuple(r.results[0][f"out_{i}_dram"] for i in range(len(_OUTS)))
```
